# Optimizing a Trainium2 kernel written in Bass

```python
import math, functools
import jax, jax.numpy as jnp
from jax import lax
import numpy as np

D_MODEL = 1024
BATCH = 1
SEQ = 256
DEPTH = 2

N_EVEN = (DEPTH + 1) // 2
N_ODD = DEPTH // 2

A_HEADS = 8
A_HEAD_DIM = 64
A_WIDTH = A_HEADS * A_HEAD_DIM
MOBA_BLOCK = 256
MOBA_TOPK = 3
Q_CHUNK = 64
ROPE_THETA = 10000.0

B_HEADS = 8
B_HEAD_K = 32
B_HEAD_V = 64
B_KEY_WIDTH = B_HEADS * B_HEAD_K
B_VAL_WIDTH = B_HEADS * B_HEAD_V
GLA_GATE_RANK = 16
GLA_GATE_NORM = 16.0
GLA_CHUNK = 64

MIX_WIDTH = A_WIDTH + B_VAL_WIDTH
EVEN_PROJ = 3 * A_WIDTH + 2 * B_KEY_WIDTH + B_VAL_WIDTH + GLA_GATE_RANK + B_VAL_WIDTH
EVEN_SPLITS = (
    A_WIDTH,
    2 * A_WIDTH,
    3 * A_WIDTH,
    3 * A_WIDTH + B_KEY_WIDTH,
    3 * A_WIDTH + 2 * B_KEY_WIDTH,
    3 * A_WIDTH + 2 * B_KEY_WIDTH + B_VAL_WIDTH,
    3 * A_WIDTH + 2 * B_KEY_WIDTH + B_VAL_WIDTH + GLA_GATE_RANK,
)

D_RNN = D_MODEL
RG_BLOCKS = 4
RG_BLOCK_W = D_RNN // RG_BLOCKS
RG_CONV = 4
LRU_C = 8.0

D_FF = 3 * D_MODEL
FFN_CONV = 3

NORM_EPS = 1e-6
NEG_INF = -1e30


def rms_norm(x, g):
    xf = x.astype(jnp.float32)
    y = xf * lax.rsqrt(jnp.mean(xf * xf, axis=-1, keepdims=True) + NORM_EPS)
    return (y * g.astype(jnp.float32)).astype(x.dtype)

def causal_dwconv(x, w, b):
    width = w.shape[0]
    seq = x.shape[1]
    xp = jnp.pad(x, ((0, 0), (width - 1, 0), (0, 0)))
    y = b
    for i in range(width):
        y = y + xp[:, i:i + seq] * w[i]
    return y

def rotary(x, pos):
    hd = x.shape[-1]
    half = hd // 2
    inv = ROPE_THETA ** (-jnp.arange(half, dtype=jnp.float32) / half)
    ang = pos.astype(jnp.float32)[:, None] * inv[None, :]
    cos, sin = jnp.cos(ang), jnp.sin(ang)
    xf = x.astype(jnp.float32)
    x1, x2 = xf[..., :half], xf[..., half:]
    return jnp.concatenate([x1 * cos - x2 * sin, x2 * cos + x1 * sin], axis=-1).astype(x.dtype)

def moba_attention(q, k, v):
    bsz, nh, seq, hd = q.shape
    nb = -(-seq // MOBA_BLOCK)
    s_pad = nb * MOBA_BLOCK
    pad = ((0, 0), (0, 0), (0, s_pad - seq), (0, 0))
    kp = jnp.pad(k, pad)
    vp = jnp.pad(v, pad)
    kb = kp.reshape(bsz, nh, nb, MOBA_BLOCK, hd)
    vb = vp.reshape(bsz, nh, nb, MOBA_BLOCK, hd)
    kmean = jnp.mean(kb.astype(jnp.float32), axis=3)
    n_sel = min(MOBA_TOPK, nb)
    scale = hd ** -0.5
    bi = jnp.arange(bsz)[:, None, None, None]
    hi = jnp.arange(nh)[None, :, None, None]
    blk_ids = jnp.arange(nb)
    n_chunks = seq // Q_CHUNK

    def one_chunk(c):
        start = c * Q_CHUNK
        qc = lax.dynamic_slice_in_dim(q, start, Q_CHUNK, axis=2).astype(jnp.float32)
        qpos = start + jnp.arange(Q_CHUNK)
        blk = start // MOBA_BLOCK
        gate = jnp.einsum('bhqd,bhnd->bhqn', qc, kmean)
        gate = jnp.where(blk_ids < blk, gate, -jnp.inf)
        _, idx = lax.top_k(gate, n_sel)
        valid = idx < blk
        kg = kb[bi, hi, idx].astype(jnp.float32)
        vg = vb[bi, hi, idx].astype(jnp.float32)
        s_sel = jnp.einsum('bhqd,bhqnkd->bhqnk', qc, kg) * scale
        s_sel = jnp.where(valid[..., None], s_sel, NEG_INF)
        own_start = blk * MOBA_BLOCK
        k_own = lax.dynamic_slice_in_dim(kp, own_start, MOBA_BLOCK, axis=2).astype(jnp.float32)
        v_own = lax.dynamic_slice_in_dim(vp, own_start, MOBA_BLOCK, axis=2).astype(jnp.float32)
        kpos = own_start + jnp.arange(MOBA_BLOCK)
        s_own = jnp.einsum('bhqd,bhkd->bhqk', qc, k_own) * scale
        s_own = jnp.where(kpos[None, :] <= qpos[:, None], s_own, NEG_INF)
        s = jnp.concatenate([s_sel.reshape(bsz, nh, Q_CHUNK, n_sel * MOBA_BLOCK), s_own], axis=-1)
        p = jax.nn.softmax(s, axis=-1)
        p_sel = p[..., :n_sel * MOBA_BLOCK].reshape(bsz, nh, Q_CHUNK, n_sel, MOBA_BLOCK)
        p_own = p[..., n_sel * MOBA_BLOCK:]
        o = (jnp.einsum('bhqnk,bhqnkd->bhqd', p_sel, vg)
             + jnp.einsum('bhqk,bhkd->bhqd', p_own, v_own))
        return o.astype(q.dtype)

    out = lax.map(one_chunk, jnp.arange(n_chunks))
    return out.transpose(1, 2, 0, 3, 4).reshape(bsz, nh, seq, hd)

def gla_attention(q, k, v, log_a):
    bsz, nh, seq, dk = q.shape
    dv = v.shape[-1]
    nc = seq // GLA_CHUNK

    def to_chunks(t):
        return t.astype(jnp.float32).reshape(bsz, nh, nc, GLA_CHUNK, t.shape[-1]).transpose(2, 0, 1, 3, 4)

    qc, kc, vc, gc = to_chunks(q), to_chunks(k), to_chunks(v), to_chunks(log_a)
    causal = jnp.tril(jnp.ones((GLA_CHUNK, GLA_CHUNK), dtype=bool))

    def step(state, inp):
        qi, ki, vi, gi = inp
        b = jnp.cumsum(gi, axis=2)
        diff = b[:, :, :, None, :] - b[:, :, None, :, :]
        decay = jnp.exp(jnp.where(causal[:, :, None], diff, -jnp.inf))
        attn = jnp.einsum('bhtd,bhsd,bhtsd->bhts', qi, ki, decay)
        o = (jnp.einsum('bhts,bhsv->bhtv', attn, vi)
             + jnp.einsum('bhtd,bhdv->bhtv', qi * jnp.exp(b), state))
        b_last = b[:, :, -1:, :]
        state = (jnp.exp(b_last[:, :, 0, :, None]) * state
                 + jnp.einsum('bhsd,bhsv->bhdv', ki * jnp.exp(b_last - b), vi))
        return state, o

    state0 = jnp.zeros((bsz, nh, dk, dv), jnp.float32)
    _, o = lax.scan(step, state0, (qc, kc, vc, gc))
    return o.transpose(1, 2, 0, 3, 4).reshape(bsz, nh, seq, dv).astype(v.dtype)

def even_mixer(x, w_in, w_gk2, b_gk2, gla_norm_g, w_out, pos):
    bsz, seq, _ = x.shape
    proj = x @ w_in
    aq, ak, av, bq, bk, bv, bgk, bog = jnp.split(proj, EVEN_SPLITS, axis=-1)

    def heads(t, n):
        return t.reshape(bsz, seq, n, -1).transpose(0, 2, 1, 3)

    o_a = moba_attention(rotary(heads(aq, A_HEADS), pos), rotary(heads(ak, A_HEADS), pos),
                         heads(av, A_HEADS))
    o_a = o_a.transpose(0, 2, 1, 3).reshape(bsz, seq, A_WIDTH)
    log_a = jax.nn.log_sigmoid((bgk @ w_gk2 + b_gk2).astype(jnp.float32)) / GLA_GATE_NORM
    o_b = gla_attention(heads(bq, B_HEADS) * (B_HEAD_K ** -0.5), heads(bk, B_HEADS),
                        heads(bv, B_HEADS), heads(log_a, B_HEADS))
    o_b = rms_norm(o_b, gla_norm_g[:, None, :])
    o_b = o_b.transpose(0, 2, 1, 3).reshape(bsz, seq, B_VAL_WIDTH) * jax.nn.silu(bog)
    return jnp.concatenate([o_a, o_b], axis=-1) @ w_out

def lru_combine(left, right):
    a1, b1 = left
    a2, b2 = right
    return a1 * a2, a2 * b1 + b2

def odd_mixer(x, w_in, conv_w, conv_b, w_a, b_a, w_x, b_x, lam, w_out):
    bsz, seq, _ = x.shape
    gate_branch, xr = jnp.split(x @ w_in, 2, axis=-1)
    xr = causal_dwconv(xr, conv_w, conv_b)
    xb = xr.reshape(bsz, seq, RG_BLOCKS, RG_BLOCK_W)
    r = jax.nn.sigmoid(jnp.einsum('bsnc,ncd->bsnd', xb, w_a).reshape(bsz, seq, D_RNN) + b_a)
    i = jax.nn.sigmoid(jnp.einsum('bsnc,ncd->bsnd', xb, w_x).reshape(bsz, seq, D_RNN) + b_x)
    log_a = (-LRU_C * r.astype(jnp.float32)) * jax.nn.softplus(-lam.astype(jnp.float32))
    a = jnp.exp(log_a)
    u = jnp.sqrt(-jnp.expm1(2.0 * log_a)) * (i * xr).astype(jnp.float32)
    _, h = lax.associative_scan(lru_combine, (a, u), axis=1)
    y = h.astype(x.dtype) * jax.nn.gelu(gate_branch)
    return y @ w_out

def conv_ffn(x, w_up, conv_w, conv_b, w_down):
    h = causal_dwconv(x @ w_up, conv_w, conv_b)
    u, g = jnp.split(h, 2, axis=-1)
    return (u * jax.nn.gelu(g)) @ w_down

def first_inputs(seed: int = 0) -> dict:
    key = jax.random.key(seed)
    ks = jax.random.split(key, 24)

    def nrm(k, shape, scale):
        return jax.random.normal(k, shape, jnp.float32) * scale

    u = jax.random.uniform(ks[14], (N_ODD, D_RNN), jnp.float32, 0.9, 0.999)
    sig = u ** (1.0 / LRU_C)
    lam = jnp.log(sig) - jnp.log1p(-sig)
    return {
        "x": nrm(ks[0], (BATCH, SEQ, D_MODEL), 1.0),
        "mix_norm_g": 1.0 + nrm(ks[1], (DEPTH, D_MODEL), 0.02),
        "ffn_norm_g": 1.0 + nrm(ks[2], (DEPTH, D_MODEL), 0.02),
        "final_norm_g": 1.0 + nrm(ks[3], (D_MODEL,), 0.02),
        "ev_w_in": nrm(ks[4], (N_EVEN, D_MODEL, EVEN_PROJ), D_MODEL ** -0.5),
        "ev_w_gk2": nrm(ks[5], (N_EVEN, GLA_GATE_RANK, B_KEY_WIDTH), GLA_GATE_RANK ** -0.5),
        "ev_b_gk2": nrm(ks[6], (N_EVEN, B_KEY_WIDTH), 0.1),
        "ev_gla_norm_g": 1.0 + nrm(ks[7], (N_EVEN, B_HEADS, B_HEAD_V), 0.02),
        "ev_w_out": nrm(ks[8], (N_EVEN, MIX_WIDTH, D_MODEL), MIX_WIDTH ** -0.5),
        "od_w_in": nrm(ks[9], (N_ODD, D_MODEL, 2 * D_RNN), D_MODEL ** -0.5),
        "od_conv_w": nrm(ks[10], (N_ODD, RG_CONV, D_RNN), RG_CONV ** -0.5),
        "od_conv_b": nrm(ks[11], (N_ODD, D_RNN), 0.01),
        "od_w_a": nrm(ks[12], (N_ODD, RG_BLOCKS, RG_BLOCK_W, RG_BLOCK_W), RG_BLOCK_W ** -0.5),
        "od_b_a": nrm(ks[13], (N_ODD, D_RNN), 0.01),
        "od_w_x": nrm(ks[15], (N_ODD, RG_BLOCKS, RG_BLOCK_W, RG_BLOCK_W), RG_BLOCK_W ** -0.5),
        "od_b_x": nrm(ks[16], (N_ODD, D_RNN), 0.01),
        "od_lambda": lam,
        "od_w_out": nrm(ks[17], (N_ODD, D_RNN, D_MODEL), D_RNN ** -0.5),
        "ffn_w_up": nrm(ks[18], (DEPTH, D_MODEL, 2 * D_FF), D_MODEL ** -0.5),
        "ffn_conv_w": nrm(ks[19], (DEPTH, FFN_CONV, 2 * D_FF), FFN_CONV ** -0.5),
        "ffn_conv_b": nrm(ks[20], (DEPTH, 2 * D_FF), 0.01),
        "ffn_w_down": nrm(ks[21], (DEPTH, D_FF, D_MODEL), D_FF ** -0.5),
    }

def first_block(x, mix_norm_g, ffn_norm_g, final_norm_g,
              ev_w_in, ev_w_gk2, ev_b_gk2, ev_gla_norm_g, ev_w_out,
              od_w_in, od_conv_w, od_conv_b, od_w_a, od_b_a, od_w_x, od_b_x, od_lambda, od_w_out,
              ffn_w_up, ffn_conv_w, ffn_conv_b, ffn_w_down):
    seq = x.shape[1]
    pos = jnp.arange(seq, dtype=jnp.int32)
    h = x
    for l in range(DEPTH):
        hn = rms_norm(h, mix_norm_g[l])
        j = l // 2
        if l % 2 == 0:
            mix = even_mixer(hn, ev_w_in[j], ev_w_gk2[j], ev_b_gk2[j], ev_gla_norm_g[j], ev_w_out[j], pos)
        else:
            mix = odd_mixer(hn, od_w_in[j], od_conv_w[j], od_conv_b[j], od_w_a[j], od_b_a[j],
                            od_w_x[j], od_b_x[j], od_lambda[j], od_w_out[j])
        h = h + mix
        h = h + conv_ffn(rms_norm(h, ffn_norm_g[l]), ffn_w_up[l], ffn_conv_w[l], ffn_conv_b[l], ffn_w_down[l])
    return rms_norm(h, final_norm_g)


_first_inputs = first_inputs


def first_inputs(seed=0):
    import zlib

    import numpy as np

    out = dict(_first_inputs(seed))
    spreads = {}
    factors = {'final_norm_g': 2.997,
     'ev_gla_norm_g': 5.694,
     'od_conv_b': 2.727,
     'od_b_a': 8.0,
     'od_b_x': 8.0,
     'ffn_conv_b': 5.009}
    for name, (base, spread) in spreads.items():
        noise = np.random.default_rng([zlib.crc32(name.encode()), seed]).standard_normal(out[name].shape)
        drawn = base * np.exp(spread * noise) if base else spread * noise
        out[name] = __import__('jax').numpy.asarray(drawn.astype(out[name].dtype))
    for name, factor in factors.items():
        out[name] = (out[name] * factor).astype(out[name].dtype)
    return out


CHUNK = 64
D_FF_2 = 2816
CONV_W = D_MODEL
CONV_K = 3
CONV_GROUPS = 16
POOL_W = D_MODEL
POOL_WINDOWS = (2, 4, 8, 16)
POOL_GROUPS = len(POOL_WINDOWS)
POOL_GC = POOL_W // POOL_GROUPS
N_BRANCH = 2
IN_COLS = 3 * CONV_W + POOL_W + N_BRANCH * D_MODEL
EPS = 1e-6


def rms_norm_2(x, g):
    xf = x.astype(jnp.float32)
    y = xf * lax.rsqrt(jnp.mean(xf * xf, axis=-1, keepdims=True) + EPS)
    return (y * g.astype(jnp.float32)).astype(x.dtype)

def swiglu(h, w_gate_up, w_down):
    gu = h @ w_gate_up
    g, u = jnp.split(gu, 2, axis=-1)
    return (jax.nn.silu(g) * u) @ w_down

def causal_depthwise_conv(u, w):
    s = u.shape[1]
    u_pad = jnp.pad(u, ((0, 0), (CONV_K - 1, 0), (0, 0)))
    y = w[0] * u_pad[:, 0:s]
    for k in range(1, CONV_K):
        y = y + w[k] * u_pad[:, k:k + s]
    return y

def trailing_mean(u, win):
    s = u.shape[1]
    cs = jnp.cumsum(u, axis=1)
    cs_shift = jnp.pad(cs, ((0, 0), (win, 0), (0, 0)))[:, :s]
    count = jnp.minimum(jnp.arange(1, s + 1), win).astype(jnp.float32)
    return (cs - cs_shift) / count[None, :, None]

def pool_mixer(p, w_pg, b_pg, scale):
    b, s, _ = p.shape
    pf = p.astype(jnp.float32).reshape(b, s, POOL_GROUPS, POOL_GC)
    pooled = jnp.stack([trailing_mean(pf[:, :, gi], win) for gi, win in enumerate(POOL_WINDOWS)], axis=2)
    d = (pooled - pf).astype(p.dtype)
    y = jnp.einsum('bsgc,gcd->bsgd', d, w_pg) + b_pg
    return y.reshape(b, s, POOL_W) * scale

def hybrid_mixer(h, w_in, b_gate, conv_w, w_conv_out, w_pg, b_pg, pool_scale, w_pool_out, w_o):
    z = h @ w_in
    b_g, c_g, v, p, gates = jnp.split(
        z, [CONV_W, 2 * CONV_W, 3 * CONV_W, 3 * CONV_W + POOL_W], axis=-1)
    y_a = (b_g * causal_depthwise_conv(c_g * v, conv_w)) @ w_conv_out
    y_p = pool_mixer(p, w_pg, b_pg, pool_scale) @ w_pool_out
    g = jax.nn.sigmoid((gates + b_gate).astype(jnp.float32)).astype(h.dtype)
    g_a, g_p = jnp.split(g, N_BRANCH, axis=-1)
    return (g_a * y_a + g_p * y_p) @ w_o

def second_inputs(seed: int = 0) -> dict:
    key = jax.random.key(seed)
    ks = jax.random.split(key, 24)
    f32 = jnp.float32

    def nrm(k, shape, fan_in):
        return jax.random.normal(k, shape, f32) * (fan_in ** -0.5)

    def gain(k, shape):
        return 1.0 + 0.05 * jax.random.normal(k, shape, f32)

    L = DEPTH
    return {
        "x": jax.random.normal(ks[0], (BATCH, SEQ, D_MODEL), f32),
        "ffn1_pre": gain(ks[1], (L, D_MODEL)),
        "ffn1_post": gain(ks[2], (L, D_MODEL)),
        "ffn1_w_gate_up": nrm(ks[3], (L, D_MODEL, 2 * D_FF_2), D_MODEL),
        "ffn1_w_down": nrm(ks[4], (L, D_FF_2, D_MODEL), D_FF_2),
        "mix_pre": gain(ks[5], (L, D_MODEL)),
        "mix_post": gain(ks[6], (L, D_MODEL)),
        "w_in": nrm(ks[7], (L, D_MODEL, IN_COLS), D_MODEL),
        "b_gate": 0.01 * jax.random.normal(ks[8], (L, N_BRANCH * D_MODEL), f32),
        "conv_w": nrm(ks[9], (L, CONV_K, CONV_W), CONV_K),
        "w_conv_out": nrm(ks[10], (L, CONV_W, D_MODEL), CONV_W),
        "w_pool_group": nrm(ks[11], (L, POOL_GROUPS, POOL_GC, POOL_GC), POOL_GC),
        "b_pool_group": 0.01 * jax.random.normal(ks[12], (L, POOL_GROUPS, POOL_GC), f32),
        "pool_scale": gain(ks[13], (L, POOL_W)),
        "w_pool_out": nrm(ks[14], (L, POOL_W, D_MODEL), POOL_W),
        "w_o": nrm(ks[15], (L, D_MODEL, D_MODEL), D_MODEL),
        "ffn2_pre": gain(ks[16], (L, D_MODEL)),
        "ffn2_post": gain(ks[17], (L, D_MODEL)),
        "ffn2_w_gate_up": nrm(ks[18], (L, D_MODEL, 2 * D_FF_2), D_MODEL),
        "ffn2_w_down": nrm(ks[19], (L, D_FF_2, D_MODEL), D_FF_2),
    }

def second_block(x, ffn1_pre, ffn1_post, ffn1_w_gate_up, ffn1_w_down,
              mix_pre, mix_post, w_in, b_gate, conv_w, w_conv_out,
              w_pool_group, b_pool_group, pool_scale, w_pool_out, w_o,
              ffn2_pre, ffn2_post, ffn2_w_gate_up, ffn2_w_down):
    for l in range(DEPTH):
        h = swiglu(rms_norm_2(x, ffn1_pre[l]), ffn1_w_gate_up[l], ffn1_w_down[l])
        x = x + 0.5 * rms_norm_2(h, ffn1_post[l])
        h = hybrid_mixer(rms_norm_2(x, mix_pre[l]), w_in[l], b_gate[l], conv_w[l],
                         w_conv_out[l], w_pool_group[l], b_pool_group[l],
                         pool_scale[l], w_pool_out[l], w_o[l])
        x = x + rms_norm_2(h, mix_post[l])
        h = swiglu(rms_norm_2(x, ffn2_pre[l]), ffn2_w_gate_up[l], ffn2_w_down[l])
        x = x + 0.5 * rms_norm_2(h, ffn2_post[l])
    return x


def setup_inputs(seed=0):
    out = dict(first_inputs(seed))
    for name, value in second_inputs(seed + 1).items():
        if name != "x":
            out[name + "_2"] = value
    return out


def reference(
    x, mix_norm_g, ffn_norm_g, final_norm_g, ev_w_in, ev_w_gk2, ev_b_gk2, ev_gla_norm_g,
    ev_w_out, od_w_in, od_conv_w, od_conv_b, od_w_a, od_b_a, od_w_x, od_b_x, od_lambda,
    od_w_out, ffn_w_up, ffn_conv_w, ffn_conv_b, ffn_w_down, ffn1_pre_2, ffn1_post_2,
    ffn1_w_gate_up_2, ffn1_w_down_2, mix_pre_2, mix_post_2, w_in_2, b_gate_2, conv_w_2,
    w_conv_out_2, w_pool_group_2, b_pool_group_2, pool_scale_2, w_pool_out_2, w_o_2, ffn2_pre_2,
    ffn2_post_2, ffn2_w_gate_up_2, ffn2_w_down_2,
):
    x = first_block(
        x, mix_norm_g, ffn_norm_g, final_norm_g, ev_w_in, ev_w_gk2, ev_b_gk2, ev_gla_norm_g,
        ev_w_out, od_w_in, od_conv_w, od_conv_b, od_w_a, od_b_a, od_w_x, od_b_x, od_lambda,
        od_w_out, ffn_w_up, ffn_conv_w, ffn_conv_b, ffn_w_down,
    )
    return second_block(
        x, ffn1_pre_2, ffn1_post_2, ffn1_w_gate_up_2, ffn1_w_down_2, mix_pre_2, mix_post_2,
        w_in_2, b_gate_2, conv_w_2, w_conv_out_2, w_pool_group_2, b_pool_group_2, pool_scale_2,
        w_pool_out_2, w_o_2, ffn2_pre_2, ffn2_post_2, ffn2_w_gate_up_2, ffn2_w_down_2,
    )


_drawn_inputs = setup_inputs


def setup_inputs(seed=0):
    import zlib

    import numpy as np

    out = dict(_drawn_inputs(seed))
    spreads = {}
    factors = {'ffn_norm_g': 4.688,
     'od_b_a': 200.0,
     'od_b_x': 200.0,
     'ffn1_pre_2': 3.134,
     'ffn1_post_2': 4.589,
     'b_gate_2': 35.186,
     'b_pool_group_2': 8.0,
     'pool_scale_2': 10.591,
     'ffn2_pre_2': 3.468,
     'ffn2_post_2': 5.11,
     'od_conv_b': 49.92,
     'od_w_a': 39.024,
     'od_w_x': 24.424,
     'od_lambda': 35.2,
     'mix_post_2': 2.769,
     'od_w_in': 8.0,
     'od_conv_w': 8.0,
     'od_w_out': 8.0}
    for name, (base, spread) in spreads.items():
        noise = np.random.default_rng([zlib.crc32(name.encode()), seed]).standard_normal(out[name].shape)
        drawn = base * np.exp(spread * noise) if base else spread * noise
        out[name] = __import__('jax').numpy.asarray(drawn.astype(out[name].dtype))
    for name, factor in factors.items():
        out[name] = (out[name] * factor).astype(out[name].dtype)
    return out
```

```python
from contextlib import ExitStack

import numpy as np
import concourse.bass as bass
from concourse import mybir
from concourse.alu_op_type import AluOpType as ALU

F32 = mybir.dt.float32
F32R = mybir.dt.float32r
U32 = mybir.dt.uint32
ACT = mybir.ActivationFunctionType
AX_X = mybir.AxisListType.X

P = 128
T = 256
D = 1024
KT = D // P
EPS = 1e-6
HEADS = 8
FF1 = 3072 // P
FF2 = 2816 // P
BLOCKS = 16
RING = 3
LAYERS2 = 2
LEVELS = 8

FIRST = [("ev_in", 13, 13), ("ev_out", 4, 4), ("up0", FF1, FF1), ("down0", 12, 4),
         ("od_xr", 4, 4), ("od_gate", 4, 4), ("od_ax", 2, 8), ("od_out", 4, 4),
         ("up1", FF1, FF1), ("down1", 12, 4)]
LAYER = [("upA", FF2, FF2), ("downA", 12, 4), ("bg", 4, 4), ("pool_in", 4, 4), ("cv", 8, 8),
         ("gates", 8, 8), ("conv_out", 4, 4), ("pool", 1, 4), ("pool_out", 4, 4),
         ("w_o", 4, 4), ("upB", FF2, FF2), ("downB", 12, 4)]
SCALED = ("ev_in", "up0", "od_xr", "od_gate", "up1", "upA", "bg", "pool_in", "cv", "gates", "upB")
C0, E0, S0 = {}, {}, {}
_c = _e = _s = 0
for _name, _nc, _ne in FIRST:
    C0[_name], E0[_name], S0[_name] = _c, _e, _s
    _c, _e, _s = _c + _nc, _e + _ne, _s + (_ne if _name in SCALED else 0)
FIRST_CHUNKS = _c
for _name, _nc, _ne in LAYER:
    C0[_name], E0[_name], S0[_name] = _c, _e, _s
    _c, _e, _s = _c + _nc, _e + _ne, _s + (_ne if _name in SCALED else 0)
LAYER_CHUNKS = _c - FIRST_CHUNKS
LAYER_EVENTS = sum(n for _, _, n in LAYER)
LAYER_SCALED = sum(n for name, _, n in LAYER if name in SCALED)
CHUNKS = FIRST_CHUNKS + LAYERS2 * LAYER_CHUNKS
STREAM = CHUNKS + RING
assert LAYER_CHUNKS % RING == 0

PAR1 = {}
_at = 0
for _name, _n in [("mix0", 8), ("mix1", 8), ("ffn0", 8), ("ffn1", 8), ("final", 8), ("bgk", 2),
                  ("glag", 4), ("odw", 32), ("odb", 8), ("ba", 8), ("bx", 8), ("lam", 8),
                  ("cw0", 144), ("cb0", 48), ("cw1", 144), ("cb1", 48)]:
    PAR1[_name] = _at
    _at += _n
NPAR1 = _at
PAR2 = {}
_at = 0
for _name, _n in [("nextA", 8), ("preA", 8), ("postA", 8), ("mpre", 8), ("mpost", 8), ("preB", 8),
                  ("postB", 8), ("bgate", 16), ("cw", 24), ("bp", 8), ("ps", 8)]:
    PAR2[_name] = _at
    _at += _n
NPAR2 = _at

SCR = 48
Q_, K_, V_, BQ, BK, BV, BOG, GK = 0, 4, 8, 12, 14, 16, 20, 24
COS, SIN, PERM, WGK, ROT = 26, 27, 28, 29, 30
PROB, VT, MBMASK, LVMASK = 26, 38, 42, 44
PT, MBUF, EBUF, OB = 0, 0, 4, 8
PRE, ACC, GEL, HID, HB = 0, 6, 12, 15, 24
YA, PIN, GA, GP, PRE2, ACC2, UU, INV = 0, 8, 16, 24, 32, 38, 41, 44
WIN, DIFF = 16, 20
XC, GB, RR, II, TMP = 0, 8, 16, 24, 32


class Signal:

    def __init__(self, sem, per_layer=0):
        self.sem, self.per_layer = sem, per_layer

    def count(self, n, layer=0):
        return (self.sem, n + layer * self.per_layer) if self.per_layer else (self.sem, n)

    def one(self):
        return self.sem, 1


class Steps:

    def __init__(self, sem, names):
        self.sem, self.names, self.at = sem, names, 0
        assert len(set(names)) == len(names)

    def after(self, name, layer=0):
        n = self.names.index(name) + 1
        return self.sem, n + layer * len(self.names)

    def did(self, name):
        assert self.names[self.at % len(self.names)] == name, (self.names[self.at % len(self.names)], name)
        self.at += 1
        return self.sem, 1


class Relay:

    def __init__(self, sem, names):
        self.sem, self.names = sem, names

    def after(self, name, layer=0):
        return self.sem, self.names.index(name) + 1 + layer * len(self.names)

    def one(self):
        return self.sem, 1


class Chunk:

    def __init__(self, phase, j, i=0, layer=0):
        c = C0[phase] + j
        self.j = j
        self.slot = c % RING
        self.n = i * RING + j
        self.turn = c // RING + i + layer * (LAYER_CHUNKS // RING)
        self.number = c + i * RING + layer * LAYER_CHUNKS
        self.event = E0[phase] + j + i * RING + layer * LAYER_EVENTS
        self.scaled = S0[phase] + j + i * RING + layer * LAYER_SCALED


def chunks(eng, phase, count, layer=0, peel=0):
    for j in range(peel):
        yield Chunk(phase, j, 0, layer)
    turns = (count - peel) // RING
    if turns > 1:
        with eng.Fori(0, turns) as i:
            for j in range(RING):
                yield Chunk(phase, peel + j, i, layer)
        peel += turns * RING
    for j in range(peel, count):
        yield Chunk(phase, j, 0, layer)


def program(nc, x_in, stream, par1_in, par2_in, ev_const, mask_const, mats, inv_in, out):
    with ExitStack() as ctx:
        def sb(name, shape, dt=F32):
            return ctx.enter_context(nc.sbuf_tensor(name, shape, dt))

        def sem(name):
            return ctx.enter_context(nc.semaphore(name))

        raw = sb("w_raw", [P, RING, BLOCKS * P])
        w_hi = sb("w_hi", [P, RING, BLOCKS * P], F32R)
        w_lo = sb("w_lo", [P, RING, BLOCKS * P], F32R)
        x = sb("x_resid", [P, KT, T])
        xs = sb("x_split", [P, KT, 2, T], F32R)
        hs = sb("h_split", [P, FF1, 2, T], F32R)
        scr = sb("scratch", [P, SCR, T])
        half = sb("half", [P, 2, T])
        sqb = sb("squares", [P, 2, T])
        sqacc = sb("square_sum", [P, 2, T])
        diag = sb("inv_rms_diagonal", [P, 2, P])
        rinv = sb("inv_rms", [P, T])
        mat = sb("matrices", [P, 3, P])
        par1 = sb("params1", [P, NPAR1])
        par2all = sb("params2", [P, LAYERS2, NPAR2])
        par2 = sb("params2_layer", [P, NPAR2])
        small = sb("small", [P, 80])
        ps = ctx.enter_context(nc.psum_tensor("psum", [P, 8, 512], F32))
        IDENT, ONES, HEADONES = mat[:, 0, :], mat[:, 1, :], mat[:, 2, :]
        eps = small[:, 0:1]
        RINV = ps[:, 6, 0:T]
        STAT = ps[:, 7, 0:2]

        def S(a, n=1):
            return scr[:, a:a + n, :]

        def S1(a):
            return scr[:, a, :]

        landed = [sem(f"chunk_landed_{s}") for s in range(RING)]
        hi_ready = sem("chunk_hi_ready")
        lo_ready = sem("chunk_lo_ready")
        chunk_done = sem("chunk_multiplied")
        pair_taken = sem("psum_pair_taken")
        const_landed = sem("const_landed")
        x_landed = sem("x_landed")
        out_landed = sem("out_landed")
        inv_landed = sem("inv_landed")
        pair_scaled = sem("pair_scaled")
        act_waited = sem("act_waited")
        pool_waited = sem("pool_waited")
        layer_par = Signal(sem("layer_params_ready"), 1)
        halved = Signal(sem("post_gains_halved"), 2)

        def round_chunk(act, slot, turn):
            act.wait_ge(landed[slot], turn * 16 + 16)
            act.activation(w_hi[:, slot, :], raw[:, slot, :], ACT.Copy).then_inc(hi_ready, 1)

        def refill_hi(act, c):
            round_chunk(act, c.slot, c.turn + 1)

        def rest_chunk(dve, slot, number):
            dve.wait_ge(hi_ready, number + 1)
            dve.tensor_tensor(w_lo[:, slot, :], raw[:, slot, :], w_hi[:, slot, :].bitcast(F32),
                              ALU.subtract).then_inc(lo_ready, 1)

        def refill_lo(dve, c):
            rest_chunk(dve, (c.slot + 2) % RING, c.number + 2)

        def multiply(pe, c, pair, src, k0, nk, first, last, ready=None, tiles=2, blk0=0,
                     signal=None, midway=None):
            for k in range(nk):
                if ready is not None:
                    pe.wait_ge(*ready(k0 + k))
                for m in range(tiles):
                    b = (blk0 + k * 2 + m) * P
                    bank = 2 * pair + m
                    pe.matmul(ps[:, bank, :], w_hi[:, c.slot, b:b + P],
                              src[:, k0 + k, :, :].rearrange("p a t -> p (a t)"),
                              start=first and k == 0, stop=False)
                    done = pe.matmul(ps[:, bank, T:2 * T], w_lo[:, c.slot, b:b + P],
                                     src[:, k0 + k, 0, :], start=False, stop=last and k == nk - 1)
                if midway is not None and k == nk // 2 - 1:
                    midway()
            if signal is not None:
                done.then_inc(*signal)

        def take_hi(act, pair, dst, tiles=2):
            return act.activation(dst, ps[:, 2 * pair:2 * pair + tiles, 0:T], ACT.Copy)

        def take_lo(dve, pair, dst, tiles=2):
            dve.tensor_tensor(dst, ps[:, 2 * pair:2 * pair + tiles, T:2 * T], dst,
                              ALU.add).then_inc(pair_taken, 1)

        def taken(event):
            return pair_taken, event + 3

        def scaled(c, back=0):
            return pair_scaled, c.scaled + (1 - back)

        def pre_tracks(name, layered=False):
            n = KT if layered else 0
            return dict(stat=Relay(sem(name + "_stat"), STAT_STEPS + ["copied"]),
                        hi=Signal(sem(name + "_hi_ready"), n), lo=Signal(sem(name + "_lo_ready"), n))

        STAT_STEPS = ["mean", "rms", "inverse", "diagonal", "rinv"]

        def mean_pe(pe, tr, summed, l):
            pe.wait_ge(*summed)
            for h in range(2):
                for a in range(2):
                    ins = pe.matmul(ps[:, 7, h:h + 1], sqacc[:, a, h * P:(h + 1) * P], ONES[:, 0:1],
                                    start=a == 0, stop=a == 1)
            ins.then_inc(*tr["stat"].one())

        def rms_act(act, tr, l):
            act.wait_ge(*tr["stat"].after("mean", l))
            act.activation(small[:, 4:6], STAT, ACT.Sqrt, bias=eps).then_inc(*tr["stat"].one())

        def rinv_dve(dve, tr, l):
            dve.wait_ge(*tr["stat"].after("rms", l))
            dve.reciprocal(small[:, 4:6], small[:, 4:6]).then_inc(*tr["stat"].one())
            dve.wait_ge(*tr["stat"].after("inverse", l))
            for h in range(2):
                ins = dve.tensor_scalar(diag[:, h, :], IDENT, small[:, 4 + h:5 + h], float(D),
                                        ALU.mult, ALU.mult)
            ins.then_inc(*tr["stat"].one())

        def rinv_pe(pe, tr, l):
            pe.wait_ge(*tr["stat"].after("diagonal", l))
            pe.matmul(RINV, ONES, diag[:, :, :].rearrange("p h t -> p (h t)"), start=True, stop=True)\
              .then_inc(*tr["stat"].one())

        def rinv_act(act, tr, l):
            act.wait_ge(*tr["stat"].after("rinv", l))
            act.activation(rinv[:, :], RINV, ACT.Copy).then_inc(*tr["stat"].one())

        def split_hi(act, tr, gain, k):
            act.activation(xs[:, bass.ds(k, 1), 0, :], x[:, bass.ds(k, 1), :], ACT.Copy,
                           scale=gain[:, bass.ds(k, 1)]).then_inc(*tr["hi"].one())

        def split_lo(dve, tr, gain, k, l):
            dve.wait_ge(*tr["hi"].count(k + 1, l))
            dve.scalar_tensor_tensor(out=xs[:, bass.ds(k, 1), 1, :], in0=x[:, bass.ds(k, 1), :],
                                     scalar=gain[:, bass.ds(k, 1)],
                                     in1=xs[:, bass.ds(k, 1), 0, :].bitcast(F32),
                                     op0=ALU.mult, op1=ALU.subtract).then_inc(*tr["lo"].one())

        def split_ready(tr, l):
            return lambda k: tr["lo"].count(k + 1, l)

        def pre_pe(pe, phases, tr, summed, l):
            for ph, n in phases:
                for c in chunks(pe, ph, n, l, peel=2):
                    pe.wait_ge(pair_taken, c.event + 1)
                    pe.wait_ge(lo_ready, c.number + 1)
                    second = isinstance(c.n, int) and c.n == 1 and ph == phases[0][0]
                    multiply(pe, c, c.slot, xs, 0, KT, True, True, split_ready(tr, l),
                             signal=(chunk_done, 1),
                             midway=(lambda: mean_pe(pe, tr, summed, l)) if second else None)
                    if second:
                        rinv_pe(pe, tr, l)

        def scale_pool(pool, phase, n, dst, l, tr=None):
            if tr is not None:
                pool.wait_ge(*tr["stat"].after("copied", l))
                pool.sem_inc(pool_waited, 1)
            for c in chunks(pool, phase, n, l):
                pool.wait_ge(*taken(c.event))
                if not isinstance(c.n, int):
                    pool.sem_inc(pool_waited, 1)
                pair = dst(c)
                pool.tensor_tensor(pair, pair, rinv[:, :].unsqueeze(1).to_broadcast([P, pair.shape[1], T]),
                                   ALU.mult).then_inc(pair_scaled, 1)

        def post_tracks(name, layered=True):
            return dict(stat=Relay(sem(name + "_stat"), STAT_STEPS),
                        y=Signal(sem(name + "_y_ready"), 8 if layered else 0),
                        xv=Signal(sem(name + "_even_x_ready"), 2 if layered else 0),
                        xg=Signal(sem(name + "_odd_x_ready"), 2 if layered else 0),
                        sq=Signal(sem(name + "_squared"), 4 if layered else 0),
                        acc=Signal(sem(name + "_summed"), 3 if layered else 0))

        def post_x(tr, g, l, final):
            if final:
                return tr["y"].count(2 * g + 2, l)
            return (tr["xg"] if g % 2 else tr["xv"]).count(g // 2 + 1, l)

        def post_act(act, tr, nxt, gain, final, l, last):
            rms_act(act, tr, l)
            refill_hi(act, last)
            for g in range(KT // 2):
                act.wait_ge(*post_x(tr, g, l, final))
                for k in (2 * g, 2 * g + 1):
                    split_hi(act, nxt, gain, k)
            for g in range(KT // 2):
                act.activation(S(HB + 2 * g, 2), x[:, 2 * g:2 * g + 2, :], ACT.Square)\
                   .then_inc(*tr["sq"].one())

        def post_dve(dve, tr, gain, nxt, ngain, final, l, next_layer):
            rinv_dve(dve, tr, l)
            dve.wait_ge(*tr["stat"].after("rinv", l))

            def lo(g):
                for k in (2 * g, 2 * g + 1):
                    split_lo(dve, nxt, ngain, k, next_layer)
            for g in range(KT // 2):
                for k in (2 * g, 2 * g + 1):
                    h = x[:, k, :] if final else S1(HB + k)
                    dve.scalar_tensor_tensor(out=h, in0=h, scalar=gain[:, k:k + 1],
                                             in1=RINV, op0=ALU.mult, op1=ALU.mult)\
                       .then_inc(*tr["y"].one())
                if not final and g % 2 == 0:
                    dve.wait_ge(*tr["y"].count(2 * g + 2, l))
                    xg = x[:, 2 * g:2 * g + 2, :]
                    dve.tensor_tensor(xg, xg, S(HB + 2 * g, 2), ALU.add).then_inc(*tr["xv"].one())
                if g:
                    lo(g - 1)
            lo(KT // 2 - 1)
            for g in range(1, KT // 2):
                dve.wait_ge(*tr["sq"].count(g + 1, l))
                if g > 1:
                    dve.wait_ge(*tr["acc"].count(g - 1, l))
                first = S(HB, 2) if g == 1 else sqacc[:, :, :]
                dve.tensor_tensor(sqacc[:, :, :], first, S(HB + 2 * g, 2), ALU.add)\
                   .then_inc(*tr["acc"].one())

        def post_pool(pool, tr, l):
            for g in (1, 3):
                pool.wait_ge(*tr["y"].count(2 * g + 2, l))
                xg = x[:, 2 * g:2 * g + 2, :]
                pool.tensor_tensor(xg, xg, S(HB + 2 * g, 2), ALU.add).then_inc(*tr["xg"].one())

        def out_tracks(name, layered):
            n = 4 if layered else 0
            return dict(half=Signal(sem(name + "_half_copied"), n), x=Signal(sem(name + "_pair_ready"), n),
                        sq=Signal(sem(name + "_squared"), n),
                        acc=Signal(sem(name + "_summed"), 5 if layered else 0))

        def groups(eng, phase, per, layer, loop=False):
            s0 = C0[phase] % RING
            if per == 1 or not loop:
                for g in range(4):
                    cs = [Chunk(phase, (g * per + q) % RING, (g * per + q) // RING, layer) for q in range(per)]
                    pair = cs[0].slot if per == 1 else (s0 + g % 2) % RING
                    yield g, cs, pair, E0[phase] + g + layer * LAYER_EVENTS
            else:
                with eng.Fori(0, 2) as i:
                    for b in range(2):
                        cs = [Chunk(phase, b * per + q, i * 2, layer) for q in range(per)]
                        yield i * 2 + b, cs, (s0 + b) % RING, E0[phase] + b + i * 2 + layer * LAYER_EVENTS

        def out_pe(pe, phase, per, src, nk, ready, l, k0=0):
            for g, cs, pair, event in groups(pe, phase, per, l, loop=True):
                pe.wait_ge(pair_taken, event + 1)
                for q, c in enumerate(cs):
                    pe.wait_ge(lo_ready, c.number + 1)
                    multiply(pe, c, pair, src, k0 + 8 * q, min(8, nk - 8 * q), q == 0,
                             q == len(cs) - 1, ready, signal=(chunk_done, 1))

        def out_act(act, phase, per, tr, dst, l, nxt=None, gain=None):
            if nxt is None:
                act.activation(small[:, 6:7], eps, ACT.Sqrt)
            for g, cs, pair, event in groups(act, phase, per, l):
                for c in cs[:-1]:
                    act.wait_ge(chunk_done, c.number + 1)
                    refill_hi(act, c)
                c = cs[-1]
                act.wait_ge(chunk_done, c.number + 1)
                take_hi(act, pair, half[:, :, :] if dst is None else S(dst + 2 * g, 2))\
                    .then_inc(*tr["half"].one())
                if g < 3:
                    refill_hi(act, c)
                if dst is None:
                    act.wait_ge(*tr["x"].count(g + 1, l))
                else:
                    act.wait_ge(*taken(event))
                if nxt is not None:
                    for t in range(2):
                        split_hi(act, nxt, gain, g * 2 + t)
                act.activation(sqb[:, :, :], x[:, 2 * g:2 * g + 2, :] if dst is None else S(dst + 2 * g, 2),
                               ACT.Square).then_inc(*tr["sq"].one())
            if nxt is not None:
                refill_hi(act, c)
            return c

        def out_dve(dve, phase, per, tr, dst, l, nxt=None, gain=None):
            dve.memset(sqacc[:, :, :], 0.0).then_inc(*tr["acc"].one())
            for g, cs, pair, event in groups(dve, phase, per, l):
                for c in cs[:-1]:
                    refill_lo(dve, c)
                c = cs[-1]
                dve.wait_ge(*tr["half"].count(g + 1, l))
                take_lo(dve, pair, half[:, :, :] if dst is None else S(dst + 2 * g, 2))
                if dst is None:
                    dve.wait_ge(*taken(event))
                    xg = x[:, 2 * g:2 * g + 2, :]
                    dve.tensor_tensor(xg, xg, half[:, :, :], ALU.add).then_inc(*tr["x"].one())
                if g < 3:
                    refill_lo(dve, c)
                if nxt is not None:
                    for t in range(2):
                        split_lo(dve, nxt, gain, g * 2 + t, l)
                    if g == 3:
                        refill_lo(dve, c)
                dve.wait_ge(*tr["acc"].count(g + 1, l))
                dve.wait_ge(*tr["sq"].count(g + 1, l))
                dve.tensor_tensor(sqacc[:, :, :], sqacc[:, :, :], sqb[:, :, :], ALU.add)\
                   .then_inc(*tr["acc"].one())
            if nxt is None:
                refill_lo(dve, c)

        def summed(tr, l=0):
            return tr["acc"].count(5, l)

        def up_tracks(name, n, layered, conv):
            m = n if layered else 0
            names = ["half", "act", "hidden", "hi", "lo"] + (["taps", "g1", "u1", "gate", "up"] if conv else [])
            return {k: Signal(sem(f"{name}_{k}_ready"), 2 * m if k == "taps" else m) for k in names}

        def up_act(act, phase, n, tr, func, conv, pre, l):
            def gate(c, prev):
                s = (c.slot - prev) % RING
                act.wait_ge(*(tr["gate"].count(c.n + 1 - prev, l) if conv else scaled(c, prev)))
                act.activation(S1(GEL + s), S1((ACC + 2 * s + 1) if conv else (PRE + 2 * s)), func)\
                   .then_inc(*tr["act"].one())

            def hi(c, prev):
                s = (c.slot - prev) % RING
                act.wait_ge(*tr["hidden"].count(c.n + 1 - prev, l))
                act.activation(hs[:, bass.ds(c.n - prev, 1), 0, :], S(HID + s), ACT.Copy)\
                   .then_inc(*tr["hi"].one())

            def taps(c):
                w, b = conv
                act.wait_ge(*scaled(c))
                for t in range(2):
                    col = c.n * 2 + t
                    act.activation(S1(ACC + 2 * c.slot + t), S1(PRE + 2 * c.slot + t), ACT.Identity,
                                   scale=w[:, bass.ds(col * 3 + 2, 1)], bias=b[:, bass.ds(col, 1)])\
                       .then_inc(*tr["taps"].one())

            def rest(c, later):
                if conv:
                    taps(c)
                else:
                    gate(c, 0)
                if later:
                    hi(c, 1)
            for c in chunks(act, phase, n, l, peel=3):
                at = c.n if isinstance(c.n, int) else n
                act.wait_ge(chunk_done, c.number + 1)
                take_hi(act, c.slot, S(PRE + 2 * c.slot, 2)).then_inc(*tr["half"].one())
                if at == 1:
                    rinv_act(act, pre, l)
                if conv and at > 1:
                    gate(c, 1)
                refill_hi(act, c)
                if at == 0:
                    chunk0 = c
                    rms_act(act, pre, l)
                    continue
                if at == 1:
                    rest(chunk0, False)
                    if conv:
                        gate(chunk0, 0)
                rest(c, True)
            if conv:
                gate(c, 0)
            hi(c, 0)

        def up_dve(dve, phase, n, tr, conv, pre, l):
            def hidden(c, prev):
                s = (c.slot - prev) % RING
                if conv:
                    dve.wait_ge(*tr["up"].count(c.n + 1 - prev, l))
                dve.wait_ge(*tr["act"].count(c.n + 1 - prev, l))
                dve.tensor_tensor(S1(HID + s), S1((ACC + 2 * s) if conv else (PRE + 2 * s + 1)),
                                  S1(GEL + s), ALU.mult).then_inc(*tr["hidden"].one())

            def lo(c, prev):
                s = (c.slot - prev) % RING
                dve.wait_ge(*tr["hi"].count(c.n + 1 - prev, l))
                dve.tensor_tensor(hs[:, bass.ds(c.n - prev, 1), 1, :], S(HID + s),
                                  hs[:, bass.ds(c.n - prev, 1), 0, :].bitcast(F32), ALU.subtract)\
                   .then_inc(*tr["lo"].one())

            def taps(c):
                def tap(t, d, after, signal):
                    dve.wait_ge(*after)
                    dve.scalar_tensor_tensor(
                        out=scr[:, ACC + 2 * c.slot + t, d:T], in0=scr[:, PRE + 2 * c.slot + t, 0:T - d],
                        scalar=conv[0][:, bass.ds((c.n * 2 + t) * 3 + 2 - d, 1)],
                        in1=scr[:, ACC + 2 * c.slot + t, d:T], op0=ALU.mult, op1=ALU.add)\
                       .then_inc(*signal.one())
                tap(1, 1, tr["taps"].count(c.n * 2 + 2, l), tr["g1"])
                tap(0, 1, tr["taps"].count(c.n * 2 + 2, l), tr["u1"])
                tap(1, 2, tr["g1"].count(c.n + 1, l), tr["gate"])
                tap(0, 2, tr["u1"].count(c.n + 1, l), tr["up"])
            for c in chunks(dve, phase, n, l, peel=3):
                at = c.n if isinstance(c.n, int) else n
                dve.wait_ge(*tr["half"].count(c.n + 1, l))
                take_lo(dve, c.slot, S(PRE + 2 * c.slot, 2))
                if at > 1:
                    hidden(c, 1)
                refill_lo(dve, c)
                if at == 0:
                    chunk0 = c
                    rinv_dve(dve, pre, l)
                    continue
                if at == 1:
                    if conv:
                        taps(chunk0)
                    hidden(chunk0, 0)
                if at > 1:
                    lo(c, 2)
                if conv:
                    taps(c)
            hidden(c, 0)
            lo(c, 1)
            lo(c, 0)

        def hs_ready(tr, l):
            return lambda k: tr["lo"].count(k + 1, l)

        G4 = range(4)
        N = {n: pre_tracks(n, n in ("normA", "normM", "normB")) for n in
             ("mixnorm0", "ffnnorm0", "mixnorm1", "ffnnorm1", "normA", "normM", "normB")}
        PN = {n: post_tracks(n, n != "final") for n in ("final", "postA", "postM", "postB")}
        O = {n: out_tracks(n, n in ("downA", "w_o", "downB")) for n in
             ("ev_out", "down0", "od_out", "down1", "downA", "w_o", "downB")}
        U = {"up0": up_tracks("up0", FF1, False, True), "up1": up_tracks("up1", FF1, False, True),
             "upA": up_tracks("upA", FF2, True, False), "upB": up_tracks("upB", FF2, True, False)}
        start_act = Steps(sem("start_act"), [f"sq{g}" for g in G4])
        start_dve = Steps(sem("start_dve"), ["eps"] + [f"acc{g}" for g in range(1, 4)])
        pe_start = sem("pe_start")
        evin_half = Signal(sem("ev_in_half_copied"))

        L = range(1, LEVELS + 1)
        ev_pe = Steps(sem("ev_pe"), ["z", "rot", "vT", "score", "pT", "pv", "bvT"] +
                      sum(([f"lv{i}a", f"lv{i}b"] for i in range(LEVELS + 1)), []) + ["gpv", "gst"])
        ev_act = Steps(sem("ev_act"), ["vt", "abs", "ex", "ln"] +
                       [f"exp{i}" for i in range(16)] + ["pt", "ohi", "bvt"] +
                       sum(([f"er{i}", f"el{i}"] for i in L), []) +
                       ["go", "gsq", "silu", "grms", "ghi"])
        ev_dve = Steps(sem("ev_dve"), ["rsin", "rcos", "rope", "z0", "z1", "mn", "g", "qs", "smask", "mx0",
                                       "mx1", "nmx", "rs", "pn0", "pn1", "pt", "olo", "azero"] +
                       sum(([f"al{i}", f"mr{i}", f"ml{i}", f"f{i}", f"sel{i - 1}a", f"sel{i - 1}b"] for i in L), []) +
                       [f"sel{LEVELS}a", f"sel{LEVELS}b", "gri"] + [f"gn{j}" for j in G4] + ["gm", "glo"])

        xr_names = []
        for g in G4:
            xr_names += [f"{t}{d}_{g}" for d in (1, 2, 3) for t in "ab"] + [f"lo{g}"]
        od_act = Steps(sem("od_act"), ["half0", "half1", "a_0", "b_0", "hi0", "a_1", "b_1", "hi1"] +
                       sum(([f"half{g}", f"a_{g}", f"b_{g}", f"hi{g}"] for g in (2, 3)), []) +
                       sum(([f"ghalf{g}", f"gelu{g}"] for g in G4), []) +
                       ["lam_ex"] +
                       sum(([f"ahalf{j}", f"r{j}", f"i{j}"] for j in range(8)), []) +
                       sum(([f"a{h}", f"tanh{h}"] for h in range(2)), []) + ["sqrt0", "sqrt1", "yhi0", "yhi1"])
        LAMN = ["l_e", "l_s", "l_r", "l_z", "l_w"] + [f"l_p{i}" for i in range(16)] + ["l_m", "l_c0", "l_c"]
        od_dve = Steps(sem("od_dve"), xr_names + ["l_abs"] + LAMN +
                       sum(([f"la{h}", f"ux{h}"] for h in range(2)), []) +
                       sum(([f"a2{h}", f"v{h}"] for h in range(2)), []) +
                       sum(([f"u{h}"] + [f"scan{h}{k}" for k in G4] + [f"y{h}"] for h in range(2)), []) +
                       ["ylo0", "ylo1"])
        ax_done = sem("ax_step_done")

        def windows():
            out_ = []
            for g in G4:
                if g:
                    out_.append(f"plo{g - 1}")
                for s in range(g + 1):
                    out_ += [f"w{g}_{s}", f"h{g}_{s}"]
            return out_ + ["plo3"]
        pool_dve = Steps(sem("pool_dve"), windows())
        pool_act = Steps(sem("pool_act"), ["phalf0"] +
                         sum(([f"phalf{g + 1}", f"phi{g}"] for g in range(3)), []) + ["phi3"])
        pool_mean = Signal(sem("pool_mean"), 4)
        pool_diff = Signal(sem("pool_diff"), 4)
        bg_half = Signal(sem("bg_half_copied"), 4)
        cv = {k: Signal(sem(f"cv_{k}"), 8) for k in ("half", "u", "tap2", "tap1", "tap0", "z", "hi", "lo")}
        gate_half = Signal(sem("gate_half_copied"), 8)
        gate_sig = Signal(sem("gate_sigmoid"), 16)
        CO = dict(half=Signal(sem("conv_out_half"), 4), ya=Signal(sem("conv_out_gated"), 4))
        pool_step = Signal(sem("pool_step_done"), 3)
        PL = {k: Signal(sem(f"pool_{k}"), 4 * (2 if k == "b" else 1)) for k in ("half", "b", "hi", "lo")}
        PO = {k: Signal(sem(f"pool_out_{k}"), 4) for k in ("half", "gated", "m", "hi", "lo")}

        def attention_pe(pe):
            pe.wait_ge(pair_scaled, 13)
            for m in range(2):
                ins = pe.matmul(ps[:, 6, m * T:(m + 1) * T], scr[0:16, WGK, m * P:(m + 1) * P],
                                scr[0:16, GK, :], start=True, stop=True)
            ins.then_inc(*ev_pe.did("z"))
            for j in range(8):
                ins = pe.matmul(ps[:, j // 2, (j % 2) * T:(j % 2 + 1) * T], scr[:, PERM, 0:P], S1(Q_ + j),
                                start=True, stop=True)
            ins.then_inc(*ev_pe.did("rot"))

            def transposed(src, name):
                for th in range(2):
                    for j in range(4):
                        ins_ = pe.transpose(ps[:, 4 + th, j * P:(j + 1) * P],
                                            scr[:, src + j, th * P:(th + 1) * P], IDENT)
                ins_.then_inc(*ev_pe.did(name))
            transposed(V_, "vT")
            pe.wait_ge(*ev_dve.after("rope"))
            pe.wait_ge(*ev_act.after("vt"))
            pe.wait_ge(*ev_dve.after("z1"))
            for h in range(HEADS):
                o = 64 * (h % 2)
                q, k = scr[o:o + 64, Q_ + h // 2, :], scr[o:o + 64, K_ + h // 2, :]
                pe.matmul(ps[:, h, 0:P], q[:, 0:P], k[:, 0:P], start=True, stop=True)
                ins = pe.matmul(ps[:, h, P:3 * P], q[:, P:T], k, start=True, stop=True)
            ins.then_inc(*ev_pe.did("score"))
            pe.wait_ge(*ev_dve.after("pn1"))
            prob = S(PROB, 12).rearrange("p a t -> p (a t)").rearrange("p (h c) -> p h c", h=HEADS)
            for h in range(HEADS):
                for b in range(3):
                    ins = pe.transpose(ps[:, h, b * P:(b + 1) * P], prob[:, h, b * P:(b + 1) * P], IDENT)
            ins.then_inc(*ev_pe.did("pT"))
            pe.wait_ge(*ev_act.after("pt"))
            pe.wait_ge(*ev_dve.after("pt"))
            values_pe(pe, S(PT, 12), "pv")
            pe.wait_ge(*ev_act.after("ohi"))
            pe.wait_ge(*ev_dve.after("olo"))
            transposed(BV, "bvT")
            pe.wait_ge(*ev_act.after("bvt"))
            for i in range(LEVELS + 1):
                for half_, b0 in (("a", 0), ("b", 4)):
                    if i:
                        pe.wait_ge(*ev_dve.after(f"ml{i}"))
                        pe.wait_ge(*ev_dve.after(f"sel{i - 1}{half_}"))
                    else:
                        pe.wait_ge(*ev_dve.after("qs"))
                    for h in range(b0, b0 + 4):
                        o, t = 32 * (h % 4), h // 4
                        ks = scr[o:o + 32, BK + t, :]
                        qs = scr[o:o + 32, BQ + t, :]
                        if i:
                            ks = qs = scr[o:o + 32, MBUF + 2 * (i % 2) + t, :]
                        if i == LEVELS:
                            ins = pe.matmul(ps[:, h, 0:P], ks[:, 0:P], qs[:, P:T], start=True, stop=True)
                        else:
                            for b in range(2):
                                ins = pe.matmul(ps[:, h, b * P:(b + 1) * P], ks[:, b * P:(b + 1) * P],
                                                qs[:, b * P:(b + 1) * P], start=True, stop=True)
                    ins.then_inc(*ev_pe.did(f"lv{i}{half_}"))
            pe.wait_ge(*ev_dve.after(f"sel{LEVELS}b"))
            values_pe(pe, S(PROB, 12), "gpv")
            pe.wait_ge(*ev_act.after("gsq"))
            for b in range(2):
                ins = pe.matmul(ps[:, 4 + b, :], HEADONES,
                                S(EBUF + 2 * b, 2).rearrange("p a t -> p (a t)"), start=True, stop=True)
            ins.then_inc(*ev_pe.did("gst"))

        def values_pe(pe, weights_t, name):
            wt = weights_t.rearrange("p a t -> p (a t)").rearrange("p (h c) -> p h c", h=HEADS)
            vt = S(VT, 4).rearrange("p (a b) t -> p a (b t)", a=2)
            for h in range(HEADS):
                o = 64 * (h % 2)
                v0, v1 = vt[:, 0, h * 64:h * 64 + 64], vt[:, 1, h * 64:h * 64 + 64]
                pe.matmul(ps[o:o + 64, h // 2, 0:T], v0, wt[:, h, 0:T], start=True, stop=False)
                ins = pe.matmul(ps[o:o + 64, h // 2, P:T], v1, wt[:, h, T:T + P], start=False, stop=True)
            ins.then_inc(*ev_pe.did(name))

        def attention_act(act):
            vt = S(VT, 4).rearrange("p (a b) t -> p a (b t)", a=2)
            act.wait_ge(*ev_pe.after("vT"))
            act.activation(vt, ps[:, 4:6, :], ACT.Copy).then_inc(*ev_act.did("vt"))
            act.wait_ge(*ev_dve.after("z1"))
            act.activation(half[:, :, :], S(GK, 2), ACT.Abs).then_inc(*ev_act.did("abs"))
            act.wait_ge(*ev_act.after("abs"))
            act.activation(half[:, :, :], half[:, :, :], ACT.Exp, scale=-1.0).then_inc(*ev_act.did("ex"))
            act.wait_ge(*ev_act.after("ex"))
            act.activation(half[:, :, :], half[:, :, :], ACT.Ln, bias=small[:, 1:2]).then_inc(*ev_act.did("ln"))
            prob = S(PROB, 12).rearrange("p a t -> p (a t)").rearrange("p (h c) -> p h c", h=HEADS)
            act.wait_ge(*ev_dve.after("nmx"))
            for i in range(16):
                h, lo_, hi_ = i % 8, P * (i // 8), P + 2 * P * (i // 8)
                act.activation(prob[:, h, lo_:hi_], prob[:, h, lo_:hi_], ACT.Exp, scale=0.125,
                               bias=small[:, 16 + i:17 + i], accum_out=small[:, 32 + i:33 + i])\
                   .then_inc(*ev_act.did(f"exp{i}"))
            pt = S(PT, 12).rearrange("p a t -> p (a t)").rearrange("p (h c) -> p h c", h=HEADS)
            act.wait_ge(*ev_pe.after("pT"))
            act.activation(pt[:, 0:4, :], ps[:, 0:4, 0:3 * P], ACT.Copy).then_inc(*ev_act.did("pt"))
            act.wait_ge(*ev_pe.after("pv"))
            act.activation(hs[:, 0:4, 0, :], ps[:, 0:4, 0:T], ACT.Copy).then_inc(*ev_act.did("ohi"))
            act.wait_ge(*ev_pe.after("bvT"))
            act.activation(vt, ps[:, 4:6, :], ACT.Copy).then_inc(*ev_act.did("bvt"))
            for i in L:
                n = 2 ** (i - 1)
                F = S(GK, 2).rearrange("p a (b s n) -> p (a b) s n", s=2, n=n)
                E = S(EBUF + 2 * (i % 2), 2).rearrange("p a (b s n) -> p (a b) s n", s=2, n=n)
                act.wait_ge(*ev_dve.after(f"al{i}"))
                act.activation(E[:, :, 1, :], F[:, :, 1, :], ACT.Exp).then_inc(*ev_act.did(f"er{i}"))
                act.activation(E[:, :, 0, :], E[:, :, 0, :], ACT.Exp).then_inc(*ev_act.did(f"el{i}"))
            act.wait_ge(*ev_pe.after("gpv"))
            act.activation(S(OB, 4), ps[:, 0:4, 0:T], ACT.Copy).then_inc(*ev_act.did("go"))
            act.activation(S(EBUF, 4), ps[:, 0:4, 0:T], ACT.Square).then_inc(*ev_act.did("gsq"))
            act.activation(S(BOG, 4), S(BOG, 4), ACT.Silu).then_inc(*ev_act.did("silu"))
            act.wait_ge(*ev_pe.after("gst"))
            act.activation(S(MBUF, 4).rearrange("p (a b) t -> p a (b t)", a=2), ps[:, 4:6, :], ACT.Sqrt,
                           bias=eps).then_inc(*ev_act.did("grms"))
            act.wait_ge(*ev_dve.after("gm"))
            act.activation(hs[:, 4:8, 0, :], S(OB, 4), ACT.Copy).then_inc(*ev_act.did("ghi"))

        def odd_act(act):
            A = od_act

            def xr_rest(g):
                c = Chunk("od_xr", g)
                act.wait_ge(*scaled(c))
                for t, nm in enumerate("ab"):
                    k = 2 * g + t
                    act.activation(S1(XC + k), S1(TMP + 2 * c.slot + t), ACT.Identity,
                                   scale=par1[:, PAR1["odw"] + 4 * k + 3:PAR1["odw"] + 4 * k + 4],
                                   bias=par1[:, PAR1["odb"] + k:PAR1["odb"] + k + 1]).then_inc(*A.did(f"{nm}_{g}"))
                act.wait_ge(*od_dve.after(f"b3_{g}"))
                act.activation(hs[:, 8 + 2 * g:10 + 2 * g, 0, :], S(XC + 2 * g, 2), ACT.Copy)\
                   .then_inc(*A.did(f"hi{g}"))
            for g in G4:
                c = Chunk("od_xr", g)
                act.wait_ge(chunk_done, c.number + 1)
                take_hi(act, c.slot, S(TMP + 2 * c.slot, 2)).then_inc(*A.did(f"half{g}"))
                if g == 1:
                    rinv_act(act, N["mixnorm1"], 0)
                refill_hi(act, c)
                if g == 0:
                    rms_act(act, N["mixnorm1"], 0)
                    continue
                if g == 1:
                    xr_rest(0)
                xr_rest(g)
            for g in G4:
                c = Chunk("od_gate", g)
                act.wait_ge(chunk_done, c.number + 1)
                take_hi(act, c.slot, S(GB + 2 * g, 2)).then_inc(*A.did(f"ghalf{g}"))
                refill_hi(act, c)
                act.wait_ge(*scaled(c))
                act.activation(S(GB + 2 * g, 2), S(GB + 2 * g, 2), ACT.Gelu_apprx_tanh)\
                   .then_inc(*A.did(f"gelu{g}"))
            act.wait_ge(*od_dve.after("l_abs"))
            act.activation(small[:, 56:64], small[:, 48:56], ACT.Exp, scale=-1.0).then_inc(*A.did("lam_ex"))
            for j in range(8):
                q, s = divmod(j, 4)
                c = Chunk("od_ax", q)
                pair = (c.slot + s) % RING
                if s == 3:
                    act.wait_ge(chunk_done, c.number + 1)
                else:
                    act.wait_ge(ax_done, 3 * q + s + 1)
                take_hi(act, pair, S(TMP + 2 * pair, 2)).then_inc(*A.did(f"ahalf{j}"))
                if s == 3:
                    refill_hi(act, c)
                act.wait_ge(*taken(E0["od_ax"] + j))
                for t, (dst, b, nm) in enumerate(((RR, "ba", "r"), (II, "bx", "i"))):
                    act.activation(S1(dst + j), S1(TMP + 2 * pair + t), ACT.Sigmoid,
                                   bias=par1[:, PAR1[b] + j:PAR1[b] + j + 1]).then_inc(*A.did(f"{nm}{j}"))
            for h in range(2):
                act.wait_ge(*od_dve.after(f"la{h}"))
                act.activation(S(TMP + 4 * h, 4), S(RR + 4 * h, 4), ACT.Exp).then_inc(*A.did(f"a{h}"))
                act.activation(S(RR + 4 * h, 4), S(RR + 4 * h, 4), ACT.Tanh, scale=-1.0)\
                   .then_inc(*A.did(f"tanh{h}"))
            for h in range(2):
                act.wait_ge(*od_dve.after(f"v{h}"))
                act.activation(S(RR + 4 * h, 4), S(RR + 4 * h, 4), ACT.Sqrt).then_inc(*A.did(f"sqrt{h}"))
            for h in range(2):
                act.wait_ge(*od_dve.after(f"y{h}"))
                act.activation(hs[:, 4 * h:4 * h + 4, 0, :], S(GB + 4 * h, 4), ACT.Copy)\
                   .then_inc(*A.did(f"yhi{h}"))

        def hybrid_act(act, l):
            def pooled_hi(g):
                act.wait_ge(*pool_diff.count(g + 1, l))
                act.activation(hs[:, 8 + 2 * g:10 + 2 * g, 0, :], S(DIFF, 2), ACT.Copy)\
                   .then_inc(*pool_act.did(f"phi{g}"))
            for g in G4:
                c = Chunk("bg", g, 0, l)
                act.wait_ge(chunk_done, c.number + 1)
                take_hi(act, c.slot, S(YA + 2 * g, 2)).then_inc(*bg_half.one())
                if g == 1:
                    rinv_act(act, N["normM"], l)
                refill_hi(act, c)
                if g == 0:
                    rms_act(act, N["normM"], l)
            for g in G4:
                c = Chunk("pool_in", g, 0, l)
                act.wait_ge(chunk_done, c.number + 1)
                take_hi(act, c.slot, S(PIN + 2 * g, 2)).then_inc(*pool_act.did(f"phalf{g}"))
                refill_hi(act, c)
                if g:
                    pooled_hi(g - 1)

            def hi(c, prev):
                s = (c.slot - prev) % RING
                act.wait_ge(*cv["z"].count(c.n + 1 - prev, l))
                act.activation(hs[:, bass.ds(c.n - prev, 1), 0, :], S(ACC2 + s), ACT.Copy)\
                   .then_inc(*cv["hi"].one())
            def tap2(c, prev):
                s = (c.slot - prev) % RING
                act.wait_ge(*cv["u"].count(c.n + 1 - prev, l))
                act.activation(S1(ACC2 + s), S1(UU + s), ACT.Copy,
                               scale=par2[:, bass.ds((c.n - prev) * 3 + (PAR2["cw"] + 2), 1)])\
                   .then_inc(*cv["tap2"].one())
            for c in chunks(act, "cv", 8, l, peel=2):
                at = c.n if isinstance(c.n, int) else 8
                act.wait_ge(chunk_done, c.number + 1)
                take_hi(act, c.slot, S(PRE2 + 2 * c.slot, 2)).then_inc(*cv["half"].one())
                refill_hi(act, c)
                if at == 0:
                    pooled_hi(3)
                if at >= 1:
                    tap2(c, 1)
                if at >= 2:
                    hi(c, 2)
            tap2(c, 0)
            hi(c, 1)
            hi(c, 0)
            for c in chunks(act, "gates", 8, l):
                act.wait_ge(chunk_done, c.number + 1)
                take_hi(act, c.slot, S(PRE2 + 2 * c.slot, 2)).then_inc(*gate_half.one())
                refill_hi(act, c)
                act.wait_ge(*scaled(c))
                for t, dst in enumerate((GA, GP)):
                    act.activation(scr[:, bass.ds(c.n + dst, 1), :], S(PRE2 + 2 * c.slot + t), ACT.Sigmoid,
                                   bias=par2[:, bass.ds(c.n + (PAR2["bgate"] + 8 * t), 1)])\
                       .then_inc(*gate_sig.one())
            for g in G4:
                c = Chunk("conv_out", g, 0, l)
                act.wait_ge(chunk_done, c.number + 1)
                take_hi(act, c.slot, S(YA + 2 * g, 2)).then_inc(*CO["half"].one())
                refill_hi(act, c)
            c = Chunk("pool", 0, 0, l)
            for g in G4:
                pair = (c.slot + g) % RING
                if g == 3:
                    act.wait_ge(chunk_done, c.number + 1)
                else:
                    act.wait_ge(*pool_step.count(g + 1, l))
                take_hi(act, pair, S(PRE2 + 2 * pair, 2)).then_inc(*PL["half"].one())
                if g == 3:
                    refill_hi(act, c)
                act.wait_ge(*PL["b"].count(2 * g + 2, l))
                act.activation(hs[:, 16 + 2 * g:18 + 2 * g, 0, :], S(PRE2 + 2 * pair, 2), ACT.Copy)\
                   .then_inc(*PL["hi"].one())
            for g in G4:
                c = Chunk("pool_out", g, 0, l)
                act.wait_ge(chunk_done, c.number + 1)
                take_hi(act, c.slot, S(PRE2 + 2 * c.slot, 2)).then_inc(*PO["half"].one())
                refill_hi(act, c)
                act.wait_ge(*PO["m"].count(g + 1, l))
                act.activation(hs[:, 2 * g:2 * g + 2, 0, :], S(YA + 2 * g, 2), ACT.Copy)\
                   .then_inc(*PO["hi"].one())

        def attention_dve(dve):
            V = ev_dve

            def b8(tile_ap):
                return tile_ap.to_broadcast([P, 8, T])
            dve.wait_ge(*ev_pe.after("rot"))
            dve.tensor_tensor(S(ROT, 8).rearrange("p (a b) t -> p a b t", b=2),
                              ps[:, 0:4, :].rearrange("p a (b t) -> p a b t", b=2),
                              S(SIN).unsqueeze(1).to_broadcast([P, 4, 2, T]), ALU.mult)\
               .then_inc(*V.did("rsin"))
            dve.tensor_tensor(S(Q_, 8), S(Q_, 8), b8(S(COS)), ALU.mult).then_inc(*V.did("rcos"))
            dve.wait_ge(*V.after("rcos"))
            dve.tensor_tensor(S(Q_, 8), S(Q_, 8), S(ROT, 8), ALU.add).then_inc(*V.did("rope"))
            dve.wait_ge(*ev_pe.after("z"))
            for m in range(2):
                dve.tensor_scalar(S1(GK + m), ps[:, 6, m * T:(m + 1) * T],
                                  par1[:, PAR1["bgk"] + m:PAR1["bgk"] + m + 1], None, ALU.add)\
                   .then_inc(*V.did(f"z{m}"))
            dve.wait_ge(*ev_act.after("abs"))
            dve.tensor_scalar(S(GK, 2), S(GK, 2), 0.0, 1.0 / 16, ALU.min, ALU.mult).then_inc(*V.did("mn"))
            dve.wait_ge(*V.after("mn"))
            dve.wait_ge(*ev_act.after("ln"))
            dve.scalar_tensor_tensor(out=S(GK, 2), in0=half[:, :, :], scalar=-1.0 / 16, in1=S(GK, 2),
                                     op0=ALU.mult, op1=ALU.add).then_inc(*V.did("g"))
            dve.tensor_scalar(S(BQ, 2), S(BQ, 2), 32 ** -0.5, None, ALU.mult).then_inc(*V.did("qs"))
            prob = S(PROB, 12).rearrange("p a t -> p (a t)").rearrange("p (h c) -> p h c", h=HEADS)
            mb = S(MBMASK, 2).rearrange("p a t -> p (a t)")[:, 0:3 * P]
            dve.wait_ge(*ev_pe.after("score"))
            dve.tensor_tensor(prob, ps[:, :, 0:3 * P], mb.unsqueeze(1).to_broadcast([P, 8, 3 * P]), ALU.add)\
               .then_inc(*V.did("smask"))
            dve.wait_ge(*V.after("smask"))
            dve.reduce_max(small[:, 16:24], prob[:, :, 0:P], AX_X).then_inc(*V.did("mx0"))
            dve.reduce_max(small[:, 24:32], prob[:, :, P:3 * P], AX_X).then_inc(*V.did("mx1"))
            dve.wait_ge(*V.after("mx1"))
            dve.tensor_scalar(small[:, 16:32], small[:, 16:32], -0.125, None, ALU.mult).then_inc(*V.did("nmx"))
            dve.wait_ge(*ev_act.after("exp15"))
            dve.reciprocal(small[:, 32:48], small[:, 32:48]).then_inc(*V.did("rs"))
            dve.wait_ge(*V.after("rs"))
            for i, (a, b) in enumerate(((0, P), (P, 3 * P))):
                dve.tensor_tensor(prob[:, :, a:b], prob[:, :, a:b],
                                  small[:, 32 + 8 * i:40 + 8 * i].unsqueeze(2).to_broadcast([P, 8, b - a]),
                                  ALU.mult).then_inc(*V.did(f"pn{i}"))
            pt = S(PT, 12).rearrange("p a t -> p (a t)").rearrange("p (h c) -> p h c", h=HEADS)
            dve.wait_ge(*ev_pe.after("pT"))
            dve.tensor_copy(pt[:, 4:8, :], ps[:, 4:8, 0:3 * P]).then_inc(*V.did("pt"))
            dve.wait_ge(*ev_act.after("ohi"))
            dve.tensor_tensor(hs[:, 0:4, 1, :], ps[:, 0:4, 0:T], hs[:, 0:4, 0, :].bitcast(F32), ALU.subtract)\
               .then_inc(*V.did("olo"))
            dve.memset(S(PROB, 12), 0.0).then_inc(*V.did("azero"))
            lv = S(LVMASK, 4).bitcast(U32).rearrange("p a t -> p (a t)").rearrange("p (i c) -> p i c", c=P)

            def select(i):
                for half_, b0 in (("a", 0), ("b", 4)):
                    dve.wait_ge(*ev_pe.after(f"lv{i}{half_}"))
                    if i == LEVELS:
                        ins = dve.tensor_copy(prob[:, b0:b0 + 4, P:2 * P], ps[:, b0:b0 + 4, 0:P])
                    else:
                        dst = prob[:, b0:b0 + 4, :].rearrange("p h (b t) -> p h b t", t=P)[:, :, 0:3:2, :]
                        ins = dve.copy_predicated(
                            dst, lv[:, i, :].unsqueeze(1).unsqueeze(1).to_broadcast([P, 4, 2, P]),
                            ps[:, b0:b0 + 4, 0:2 * P].rearrange("p h (b t) -> p h b t", t=P))
                    ins.then_inc(*V.did(f"sel{i}{half_}"))
            for i in L:
                n = 2 ** (i - 1)

                def halves(ap):
                    return ap.rearrange("p a (b s n) -> p (a b) s n", s=2, n=n)
                F, E = halves(S(GK, 2)), halves(S(EBUF + 2 * (i % 2), 2))
                M, Q, K = halves(S(MBUF + 2 * (i % 2), 2)), halves(S(BQ, 2)), halves(S(BK, 2))
                end = F[:, :, 0, n - 1:n].to_broadcast([P, 2 * T // (2 * n), n])
                if i == 1:
                    dve.wait_ge(*ev_pe.after("pv"))
                    dve.wait_ge(*V.after("azero"))
                dve.wait_ge(*(V.after(f"f{i - 1}") if i > 1 else V.after("g")))
                dve.tensor_tensor(E[:, :, 0, :], end, F[:, :, 0, :], ALU.subtract).then_inc(*V.did(f"al{i}"))
                if i > 2:
                    dve.wait_ge(*ev_pe.after(f"lv{i - 2}b"))
                dve.wait_ge(*ev_act.after(f"er{i}"))
                dve.tensor_tensor(M[:, :, 1, :], E[:, :, 1, :], Q[:, :, 1, :], ALU.mult).then_inc(*V.did(f"mr{i}"))
                dve.wait_ge(*ev_act.after(f"el{i}"))
                dve.tensor_tensor(M[:, :, 0, :], E[:, :, 0, :], K[:, :, 0, :], ALU.mult).then_inc(*V.did(f"ml{i}"))
                dve.tensor_tensor(F[:, :, 1, :], F[:, :, 1, :], end, ALU.add).then_inc(*V.did(f"f{i}"))
                select(i - 1)
            select(LEVELS)
            dve.wait_ge(*ev_act.after("grms"))
            dve.reciprocal(S(MBUF, 4), S(MBUF, 4)).then_inc(*V.did("gri"))
            dve.wait_ge(*V.after("gri"))
            for j in G4:
                g = PAR1["glag"] + j
                dve.scalar_tensor_tensor(out=S1(OB + j), in0=S1(OB + j), scalar=par1[:, g:g + 1],
                                         in1=S1(MBUF + j), op0=ALU.mult, op1=ALU.mult).then_inc(*V.did(f"gn{j}"))
            dve.wait_ge(*V.after("gn3"))
            dve.tensor_tensor(S(OB, 4), S(OB, 4), S(BOG, 4), ALU.mult).then_inc(*V.did("gm"))
            dve.wait_ge(*ev_act.after("ghi"))
            dve.tensor_tensor(hs[:, 4:8, 1, :], S(OB, 4), hs[:, 4:8, 0, :].bitcast(F32), ALU.subtract)\
               .then_inc(*V.did("glo"))

        def odd_dve(dve):
            V = od_dve
            def xr_rest(g):
                c = Chunk("od_xr", g)
                dve.wait_ge(*od_act.after(f"b_{g}"))
                for d in (1, 2, 3):
                    for t, nm in enumerate("ab"):
                        k = 2 * g + t
                        if d > 1:
                            dve.wait_ge(*V.after(f"{nm}{d - 1}_{g}"))
                        w = PAR1["odw"] + 4 * k + 3 - d
                        dve.scalar_tensor_tensor(out=scr[:, XC + k, d:T], in0=scr[:, TMP + 2 * c.slot + t, 0:T - d],
                                                 scalar=par1[:, w:w + 1], in1=scr[:, XC + k, d:T],
                                                 op0=ALU.mult, op1=ALU.add).then_inc(*V.did(f"{nm}{d}_{g}"))
                dve.wait_ge(*od_act.after(f"hi{g}"))
                dve.tensor_tensor(hs[:, 8 + 2 * g:10 + 2 * g, 1, :], S(XC + 2 * g, 2),
                                  hs[:, 8 + 2 * g:10 + 2 * g, 0, :].bitcast(F32), ALU.subtract)\
                   .then_inc(*V.did(f"lo{g}"))
            for g in G4:
                c = Chunk("od_xr", g)
                dve.wait_ge(*od_act.after(f"half{g}"))
                take_lo(dve, c.slot, S(TMP + 2 * c.slot, 2))
                refill_lo(dve, c)
                if g == 0:
                    rinv_dve(dve, N["mixnorm1"], 0)
                    continue
                if g == 1:
                    xr_rest(0)
                xr_rest(g)
            for g in G4:
                c = Chunk("od_gate", g)
                dve.wait_ge(*od_act.after(f"ghalf{g}"))
                take_lo(dve, c.slot, S(GB + 2 * g, 2))
                refill_lo(dve, c)
            lam = par1[:, PAR1["lam"]:PAR1["lam"] + 8]
            e, z, w, p, cc, ab = (small[:, a:a + 8] for a in (56, 64, 72, 16, 24, 48))
            dve.scalar_tensor_tensor(out=ab, in0=lam, scalar=-1.0, in1=lam, op0=ALU.mult, op1=ALU.max)\
               .then_inc(*V.did("l_abs"))

            def step(name, ins):
                ins.then_inc(*V.did(name))
                dve.wait_ge(*V.after(name))
            dve.wait_ge(*od_act.after("lam_ex"))
            step("l_e", dve.tensor_scalar(z, e, 2.0, None, ALU.add))
            step("l_s", dve.reciprocal(z, z))
            step("l_r", dve.tensor_tensor(z, z, e, ALU.mult))
            step("l_z", dve.tensor_tensor(w, z, z, ALU.mult))
            step("l_w", dve.memset(p, 1.0 / 17))
            for i in range(8):
                step(f"l_p{2 * i}", dve.tensor_tensor(p, p, w, ALU.mult))
                step(f"l_p{2 * i + 1}", dve.tensor_scalar(p, p, 1.0 / (15 - 2 * i), None, ALU.add))
            step("l_m", dve.tensor_tensor(p, p, z, ALU.mult))
            step("l_c0", dve.tensor_scalar(cc, lam, -1.0, 0.0, ALU.mult, ALU.max))
            step("l_c", dve.scalar_tensor_tensor(out=cc, in0=p, scalar=2.0, in1=cc, op0=ALU.mult, op1=ALU.add))
            for j in range(8):
                q, s = divmod(j, 4)
                c = Chunk("od_ax", q)
                pair = (c.slot + s) % RING
                dve.wait_ge(*od_act.after(f"ahalf{j}"))
                take_lo(dve, pair, S(TMP + 2 * pair, 2))
                if s == 3:
                    refill_lo(dve, c)
            for h in range(2):
                dve.wait_ge(*od_act.after(f"i7"))
                r4 = S(RR + 4 * h, 4)
                dve.scalar_tensor_tensor(out=r4, in0=r4, scalar=-8.0,
                                         in1=cc[:, 4 * h:4 * h + 4].unsqueeze(2).to_broadcast([P, 4, T]),
                                         op0=ALU.mult, op1=ALU.mult).then_inc(*V.did(f"la{h}"))
                dve.tensor_tensor(S(II + 4 * h, 4), S(II + 4 * h, 4), S(XC + 4 * h, 4), ALU.mult)\
                   .then_inc(*V.did(f"ux{h}"))
            for h in range(2):
                dve.wait_ge(*od_act.after(f"tanh{h}"))
                dve.wait_ge(*V.after("ux1"))
                dve.tensor_tensor(S(XC + 4 * h, 4), S(TMP + 4 * h, 4), S(TMP + 4 * h, 4), ALU.mult)\
                   .then_inc(*V.did(f"a2{h}"))
                dve.wait_ge(*V.after(f"a2{h}"))
                dve.scalar_tensor_tensor(out=S(RR + 4 * h, 4), in0=S(XC + 4 * h, 4), scalar=1.0,
                                         in1=S(RR + 4 * h, 4), op0=ALU.add, op1=ALU.mult).then_inc(*V.did(f"v{h}"))
            for h in range(2):
                dve.wait_ge(*od_act.after(f"sqrt{h}"))
                dve.tensor_tensor(S(II + 4 * h, 4), S(II + 4 * h, 4), S(RR + 4 * h, 4), ALU.mult)\
                   .then_inc(*V.did(f"u{h}"))
                dve.wait_ge(*V.after(f"u{h}"))
                for k in G4:
                    t = 4 * h + k
                    dve.tensor_tensor_scan(S1(XC + t), S1(TMP + t), S1(II + t), 0.0, ALU.mult, ALU.add)\
                       .then_inc(*V.did(f"scan{h}{k}"))
                dve.wait_ge(*V.after(f"scan{h}3"))
                dve.tensor_tensor(S(GB + 4 * h, 4), S(GB + 4 * h, 4), S(XC + 4 * h, 4), ALU.mult)\
                   .then_inc(*V.did(f"y{h}"))
            for h in range(2):
                dve.wait_ge(*od_act.after(f"yhi{h}"))
                dve.tensor_tensor(hs[:, 4 * h:4 * h + 4, 1, :], S(GB + 4 * h, 4),
                                  hs[:, 4 * h:4 * h + 4, 0, :].bitcast(F32), ALU.subtract)\
                   .then_inc(*V.did(f"ylo{h}"))

        def pool_means(pool, l):
            for g in G4:
                c = Chunk("pool_in", g, 0, l)
                pool.wait_ge(*taken(c.event))
                pair = S(PIN + 2 * g, 2)
                pool.tensor_tensor(pair, pair, rinv[:, :].unsqueeze(1).to_broadcast([P, 2, T]), ALU.mult)\
                    .then_inc(pair_scaled, 1)
                pool.wait_ge(*pool_dve.after(f"h{g}_{g}", l))
                pool.tensor_tensor(S(DIFF, 2), S(WIN + 2 * (g % 2), 2), S(INV + g).to_broadcast([P, 2, T]),
                                   ALU.mult).then_inc(*pool_mean.one())
                pool.wait_ge(*pool_mean.count(g + 1, l))
                pool.tensor_tensor(S(DIFF, 2), S(DIFF, 2), pair, ALU.subtract).then_inc(*pool_diff.one())

        def hybrid_dve(dve, l):
            def pooled_lo(g):
                dve.wait_ge(*pool_act.after(f"phi{g}", l))
                dve.tensor_tensor(hs[:, 8 + 2 * g:10 + 2 * g, 1, :], S(DIFF, 2),
                                  hs[:, 8 + 2 * g:10 + 2 * g, 0, :].bitcast(F32), ALU.subtract)\
                   .then_inc(*pool_dve.did(f"plo{g}"))
            for g in G4:
                c = Chunk("bg", g, 0, l)
                dve.wait_ge(*bg_half.count(g + 1, l))
                take_lo(dve, c.slot, S(YA + 2 * g, 2))
                refill_lo(dve, c)
                if g == 0:
                    rinv_dve(dve, N["normM"], l)
            for g in G4:
                c = Chunk("pool_in", g, 0, l)
                dve.wait_ge(*pool_act.after(f"phalf{g}", l))
                take_lo(dve, c.slot, S(PIN + 2 * g, 2))
                refill_lo(dve, c)
                if g:
                    pooled_lo(g - 1)
                dve.wait_ge(*scaled(c))
                src = S(PIN + 2 * g, 2)
                for s in range(g + 1):
                    d = 2 ** s
                    dst = S(WIN + 2 * (s % 2), 2)
                    dve.tensor_copy(dst[:, :, 0:d], src[:, :, 0:d]).then_inc(*pool_dve.did(f"w{g}_{s}"))
                    dve.tensor_tensor(dst[:, :, d:T], src[:, :, d:T], src[:, :, 0:T - d], ALU.add)\
                       .then_inc(*pool_dve.did(f"h{g}_{s}"))
                    if s < g:
                        dve.wait_ge(*pool_dve.after(f"h{g}_{s}", l))
                    src = dst

            def conv(c, prev):
                s, n = (c.slot - prev) % RING, c.n - prev
                for d, name, after in ((1, "tap1", "tap2"), (2, "tap0", "tap1")):
                    dve.wait_ge(*cv[after].count(n + 1, l))
                    dve.scalar_tensor_tensor(out=scr[:, ACC2 + s, d:T], in0=scr[:, UU + s, 0:T - d],
                                             scalar=par2[:, bass.ds(n * 3 + (PAR2["cw"] + 2 - d), 1)],
                                             in1=scr[:, ACC2 + s, d:T], op0=ALU.mult, op1=ALU.add)\
                       .then_inc(*cv[name].one())
                dve.wait_ge(*cv["tap0"].count(n + 1, l))
                dve.tensor_tensor(S(ACC2 + s), S(ACC2 + s), scr[:, bass.ds(n + YA, 1), :], ALU.mult)\
                   .then_inc(*cv["z"].one())

            def lo(c, prev):
                s = (c.slot - prev) % RING
                dve.wait_ge(*cv["hi"].count(c.n + 1 - prev, l))
                dve.tensor_tensor(hs[:, bass.ds(c.n - prev, 1), 1, :], S(ACC2 + s),
                                  hs[:, bass.ds(c.n - prev, 1), 0, :].bitcast(F32), ALU.subtract)\
                   .then_inc(*cv["lo"].one())
            for c in chunks(dve, "cv", 8, l, peel=2):
                known = c.n if isinstance(c.n, int) else 8
                if known == 1:
                    pooled_lo(3)
                dve.wait_ge(*cv["half"].count(c.n + 1, l))
                take_lo(dve, c.slot, S(PRE2 + 2 * c.slot, 2))
                refill_lo(dve, c)
                dve.wait_ge(*scaled(c))
                dve.tensor_tensor(S1(UU + c.slot), S1(PRE2 + 2 * c.slot), S1(PRE2 + 2 * c.slot + 1), ALU.mult)\
                   .then_inc(*cv["u"].one())
                if known >= 1:
                    conv(c, 1)
                if known >= 2:
                    lo(c, 2)
            conv(c, 0)
            lo(c, 1)
            lo(c, 0)
            for c in chunks(dve, "gates", 8, l):
                dve.wait_ge(*gate_half.count(c.n + 1, l))
                take_lo(dve, c.slot, S(PRE2 + 2 * c.slot, 2))
                refill_lo(dve, c)
            for g in G4:
                c = Chunk("conv_out", g, 0, l)
                dve.wait_ge(*CO["half"].count(g + 1, l))
                take_lo(dve, c.slot, S(YA + 2 * g, 2))
                if g == 0:
                    dve.wait_ge(*gate_sig.count(16, l))
                dve.wait_ge(*taken(c.event))
                dve.tensor_tensor(S(YA + 2 * g, 2), S(YA + 2 * g, 2), S(GA + 2 * g, 2), ALU.mult)\
                   .then_inc(*CO["ya"].one())
                refill_lo(dve, c)
            c = Chunk("pool", 0, 0, l)
            for g in G4:
                pair = (c.slot + g) % RING
                dve.wait_ge(*PL["half"].count(g + 1, l))
                take_lo(dve, pair, S(PRE2 + 2 * pair, 2))
                dve.wait_ge(*taken(E0["pool"] + g + l * LAYER_EVENTS))
                for t in range(2):
                    k = 2 * g + t
                    dve.tensor_scalar(S1(PRE2 + 2 * pair + t), S1(PRE2 + 2 * pair + t),
                                      par2[:, PAR2["bp"] + k:PAR2["bp"] + k + 1],
                                      par2[:, PAR2["ps"] + k:PAR2["ps"] + k + 1], ALU.add, ALU.mult)\
                       .then_inc(*PL["b"].one())
                if g == 3:
                    refill_lo(dve, c)
                dve.wait_ge(*PL["hi"].count(g + 1, l))
                dve.tensor_tensor(hs[:, 16 + 2 * g:18 + 2 * g, 1, :], S(PRE2 + 2 * pair, 2),
                                  hs[:, 16 + 2 * g:18 + 2 * g, 0, :].bitcast(F32), ALU.subtract)\
                   .then_inc(*PL["lo"].one())
            for g in G4:
                c = Chunk("pool_out", g, 0, l)
                dve.wait_ge(*PO["half"].count(g + 1, l))
                take_lo(dve, c.slot, S(PRE2 + 2 * c.slot, 2))
                dve.wait_ge(*taken(c.event))
                pre = S(PRE2 + 2 * c.slot, 2)
                dve.tensor_tensor(pre, pre, S(GP + 2 * g, 2), ALU.mult).then_inc(*PO["gated"].one())
                dve.wait_ge(*PO["gated"].count(g + 1, l))
                dve.tensor_tensor(S(YA + 2 * g, 2), S(YA + 2 * g, 2), pre, ALU.add).then_inc(*PO["m"].one())
                refill_lo(dve, c)
                dve.wait_ge(*PO["hi"].count(g + 1, l))
                dve.tensor_tensor(hs[:, 2 * g:2 * g + 2, 1, :], S(YA + 2 * g, 2),
                                  hs[:, 2 * g:2 * g + 2, 0, :].bitcast(F32), ALU.subtract)\
                   .then_inc(*PO["lo"].one())


        block = ctx.enter_context(nc.Block())

        @block.sync
        def _(sp):
            sp.dma_start(x[:, :, :], x_in).then_inc(x_landed, 16)
            for s in range(RING):
                sp.dma_start(raw[:, s, :], stream[s]).then_inc(landed[s], 16)
                if s == 0:
                    sp.dma_start(mat[:, :, :], mats).then_inc(const_landed, 16)
                    sp.dma_start(par1[:, :], par1_in).then_inc(const_landed, 16)
                    sp.dma_start(par2all[:, :, :], par2_in).then_inc(const_landed, 16)
                    sp.dma_start(S(COS, 4), ev_const).then_inc(const_landed, 16)
                    sp.dma_start(S(MBMASK, 6), mask_const).then_inc(const_landed, 16)
            with sp.Fori(1, STREAM // RING) as i:
                for s in range(RING):
                    sp.wait_ge(lo_ready, i * RING + (s - RING + 1))
                    sp.dma_start(raw[:, s, :], stream[i * RING + s]).then_inc(landed[s], 16)
            for n in range(STREAM // RING * RING, STREAM):
                sp.wait_ge(lo_ready, n - RING + 1)
                sp.dma_start(raw[:, n % RING, :], stream[n]).then_inc(landed[n % RING], 16)
            for g in (2, 3):
                sp.wait_ge(*post_x(PN["postB"], g, LAYERS2 - 1, False))
            sp.dma_start(out, x[:, :, :]).then_inc(out_landed, 16)
            sp.wait_ge(out_landed, 16)

        @block.gpsimd
        def _(pool):
            def scratch_pair(at):
                return lambda c: S(at + 2 * c.slot, 2)
            scale_pool(pool, "ev_in", 12, lambda c: scr[:, bass.ds(c.n * 2, 2), :], 0, N["mixnorm0"])
            pool.wait_ge(*taken(E0["ev_in"] + 12))
            pool.tensor_tensor(S1(GK), S1(GK), rinv[:, :], ALU.mult).then_inc(pair_scaled, 1)
            pool.wait_ge(*ev_dve.after("glo"))
            pool.dma_start(S(INV, 4), inv_in).then_inc(inv_landed, 16)
            scale_pool(pool, "up0", FF1, scratch_pair(PRE), 0, N["ffnnorm0"])
            scale_pool(pool, "od_xr", 4, scratch_pair(TMP), 0, N["mixnorm1"])
            scale_pool(pool, "od_gate", 4, lambda c: S(GB + 2 * c.j, 2), 0)
            scale_pool(pool, "up1", FF1, scratch_pair(PRE), 0, N["ffnnorm1"])
            with pool.Fori(0, LAYERS2) as l:
                scale_pool(pool, "upA", FF2, scratch_pair(PRE), l, N["normA"])
                post_pool(pool, PN["postA"], l)
                pool.wait_ge(inv_landed, 16)
                scale_pool(pool, "bg", 4, lambda c: S(YA + 2 * c.j, 2), l, N["normM"])
                pool_means(pool, l)
                scale_pool(pool, "cv", 8, scratch_pair(PRE2), l)
                scale_pool(pool, "gates", 8, scratch_pair(PRE2), l)
                post_pool(pool, PN["postM"], l)
                scale_pool(pool, "upB", FF2, scratch_pair(PRE), l, N["normB"])
                post_pool(pool, PN["postB"], l)

        @block.tensor
        def _(pe):
            pe.sem_inc(pair_taken, 2)
            pe.wait_ge(const_landed, 16 * 5)
            pre_pe(pe, [("ev_in", 12)], N["mixnorm0"], start_dve.after("acc3"), 0)
            c = Chunk("ev_in", 12)
            pe.wait_ge(pair_taken, c.event + 1)
            pe.wait_ge(lo_ready, c.number + 1)
            multiply(pe, c, c.slot, xs, 0, KT, True, True, tiles=1, signal=(chunk_done, 1))
            attention_pe(pe)
            out_pe(pe, "ev_out", 1, hs, 8,
                   lambda k: ev_dve.after("olo" if k < 4 else "glo") if isinstance(k, int) else None, 0)
            pre_pe(pe, [("up0", FF1)], N["ffnnorm0"], summed(O["ev_out"]), 0)
            out_pe(pe, "down0", 3, hs, FF1, hs_ready(U["up0"], 0), 0)
            pre_pe(pe, [("od_xr", 4), ("od_gate", 4)], N["mixnorm1"], summed(O["down0"]), 0)
            for q in range(2):
                c = Chunk("od_ax", q)
                pe.wait_ge(lo_ready, c.number + 1)
                for s in range(4):
                    j = 4 * q + s
                    pe.wait_ge(pair_taken, E0["od_ax"] + j + 1)
                    n = j // 2
                    multiply(pe, c, (c.slot + s) % RING, hs, 8 + 2 * n, 2, True, True,
                             lambda k, n=n: od_dve.after(f"lo{n}"), blk0=4 * s,
                             signal=(chunk_done if s == 3 else ax_done, 1))
            out_pe(pe, "od_out", 1, hs, 8, lambda k: od_dve.after(f"ylo{k // 4}"), 0)
            pre_pe(pe, [("up1", FF1)], N["ffnnorm1"], summed(O["od_out"]), 0)
            out_pe(pe, "down1", 3, hs, FF1, hs_ready(U["up1"], 0), 0)
            mean_pe(pe, PN["final"], summed(O["down1"]), 0)
            rinv_pe(pe, PN["final"], 0)
            with pe.Fori(0, LAYERS2) as l:
                pre_pe(pe, [("upA", FF2)], N["normA"], layer_par.count(1, l), l)
                out_pe(pe, "downA", 3, hs, FF2, hs_ready(U["upA"], l), l)
                mean_pe(pe, PN["postA"], summed(O["downA"], l), l)
                rinv_pe(pe, PN["postA"], l)
                pre_pe(pe, [("bg", 4), ("pool_in", 4), ("cv", 8), ("gates", 8)], N["normM"],
                       PN["postA"]["acc"].count(3, l), l)
                out_pe(pe, "conv_out", 1, hs, 8, lambda k: cv["lo"].count(k + 1, l), l)
                c = Chunk("pool", 0, 0, l)
                pe.wait_ge(lo_ready, c.number + 1)
                for g in G4:
                    pe.wait_ge(pair_taken, E0["pool"] + g + 1 + l * LAYER_EVENTS)
                    multiply(pe, c, (c.slot + g) % RING, hs, 8 + 2 * g, 2, True, True,
                             lambda k, g=g: pool_dve.after(f"plo{g}", l), blk0=4 * g,
                             signal=(chunk_done, 1) if g == 3 else pool_step.one())
                out_pe(pe, "pool_out", 1, hs, 8, lambda k: PL["lo"].count((k - 16) // 2 + 1, l), l, k0=16)
                out_pe(pe, "w_o", 1, hs, 8, lambda k: PO["lo"].count(k // 2 + 1, l), l)
                mean_pe(pe, PN["postM"], summed(O["w_o"], l), l)
                rinv_pe(pe, PN["postM"], l)
                pre_pe(pe, [("upB", FF2)], N["normB"], PN["postM"]["acc"].count(3, l), l)
                out_pe(pe, "downB", 3, hs, FF2, hs_ready(U["upB"], l), l)
                mean_pe(pe, PN["postB"], summed(O["downB"], l), l)
                rinv_pe(pe, PN["postB"], l)

        def gains(name, par=par1, table=PAR1):
            return par[:, table[name]:table[name] + KT]

        first_a = par2all[:, 0, PAR2["preA"]:PAR2["preA"] + KT]

        def gains2(name):
            return gains(name, par2, PAR2)

        @block.scalar
        def _(act):
            act.wait_ge(x_landed, 16)
            act.wait_ge(const_landed, 16 * 5)
            for k in range(KT):
                split_hi(act, N["mixnorm0"], gains("mix0"), k)
            round_chunk(act, 0, 0)
            for g in G4:
                if g > 1:
                    act.wait_ge(*start_dve.after(f"acc{g - 1}"))
                act.activation((sqb if g else sqacc)[:, :, :], x[:, 2 * g:2 * g + 2, :], ACT.Square)\
                   .then_inc(*start_act.did(f"sq{g}"))
                if g in (1, 2):
                    round_chunk(act, g, 0)
            act.wait_ge(*start_dve.after("eps"))
            for c in chunks(act, "ev_in", 12, peel=2):
                act.wait_ge(chunk_done, c.number + 1)
                take_hi(act, c.slot, scr[:, bass.ds(c.n * 2, 2), :]).then_inc(*evin_half.one())
                if isinstance(c.n, int) and c.n == 1:
                    rinv_act(act, N["mixnorm0"], 0)
                refill_hi(act, c)
                if isinstance(c.n, int) and c.n == 0:
                    rms_act(act, N["mixnorm0"], 0)
            c = Chunk("ev_in", 12)
            act.wait_ge(chunk_done, c.number + 1)
            take_hi(act, c.slot, S(GK), 1).then_inc(*evin_half.one())
            refill_hi(act, c)
            attention_act(act)
            out_act(act, "ev_out", 1, O["ev_out"], None, 0, N["ffnnorm0"], gains("ffn0"))
            cw, cb = PAR1["cw0"], PAR1["cb0"]
            up_act(act, "up0", FF1, U["up0"], ACT.Gelu_apprx_tanh,
                   (par1[:, cw:cw + 144], par1[:, cb:cb + 48]), N["ffnnorm0"], 0)
            out_act(act, "down0", 3, O["down0"], None, 0, N["mixnorm1"], gains("mix1"))
            odd_act(act)
            out_act(act, "od_out", 1, O["od_out"], None, 0, N["ffnnorm1"], gains("ffn1"))
            cw, cb = PAR1["cw1"], PAR1["cb1"]
            up_act(act, "up1", FF1, U["up1"], ACT.Gelu_apprx_tanh,
                   (par1[:, cw:cw + 144], par1[:, cb:cb + 48]), N["ffnnorm1"], 0)
            last = out_act(act, "down1", 3, O["down1"], None, 0)
            post_act(act, PN["final"], N["normA"], first_a, True, 0, last)
            with act.Fori(0, LAYERS2) as l:
                up_act(act, "upA", FF2, U["upA"], ACT.Silu, None, N["normA"], l)
                last = out_act(act, "downA", 3, O["downA"], HB, l)
                post_act(act, PN["postA"], N["normM"], gains2("mpre"), False, l, last)
                hybrid_act(act, l)
                last = out_act(act, "w_o", 1, O["w_o"], HB, l)
                post_act(act, PN["postM"], N["normB"], gains2("preB"), False, l, last)
                up_act(act, "upB", FF2, U["upB"], ACT.Silu, None, N["normB"], l)
                last = out_act(act, "downB", 3, O["downB"], HB, l)
                post_act(act, PN["postB"], N["normA"], gains2("nextA"), False, l, last)

        @block.vector
        def _(dve):
            dve.memset(small[:, 1:2], 1.0)
            dve.memset(small[:, 0:1], EPS).then_inc(*start_dve.did("eps"))
            dve.wait_ge(const_landed, 16 * 5)
            for k in range(KT):
                split_lo(dve, N["mixnorm0"], gains("mix0"), k, 0)
            rest_chunk(dve, 0, 0)
            for g in range(1, 4):
                dve.wait_ge(*start_act.after(f"sq{g}"))
                if g > 1:
                    dve.wait_ge(*start_dve.after(f"acc{g - 1}"))
                dve.tensor_tensor(sqacc[:, :, :], sqacc[:, :, :], sqb[:, :, :], ALU.add)\
                   .then_inc(*start_dve.did(f"acc{g}"))
                if g == 2:
                    rest_chunk(dve, 1, 1)
            for c in chunks(dve, "ev_in", 12, peel=2):
                dve.wait_ge(*evin_half.count(c.n + 1))
                take_lo(dve, c.slot, scr[:, bass.ds(c.n * 2, 2), :])
                refill_lo(dve, c)
                if isinstance(c.n, int) and c.n == 0:
                    rinv_dve(dve, N["mixnorm0"], 0)
            c = Chunk("ev_in", 12)
            dve.wait_ge(*evin_half.count(13))
            take_lo(dve, c.slot, S(GK), 1)
            refill_lo(dve, c)
            attention_dve(dve)
            out_dve(dve, "ev_out", 1, O["ev_out"], None, 0, N["ffnnorm0"], gains("ffn0"))
            cw, cb = PAR1["cw0"], PAR1["cb0"]
            up_dve(dve, "up0", FF1, U["up0"], (par1[:, cw:cw + 144], par1[:, cb:cb + 48]), N["ffnnorm0"], 0)
            out_dve(dve, "down0", 3, O["down0"], None, 0, N["mixnorm1"], gains("mix1"))
            odd_dve(dve)
            out_dve(dve, "od_out", 1, O["od_out"], None, 0, N["ffnnorm1"], gains("ffn1"))
            cw, cb = PAR1["cw1"], PAR1["cb1"]
            up_dve(dve, "up1", FF1, U["up1"], (par1[:, cw:cw + 144], par1[:, cb:cb + 48]), N["ffnnorm1"], 0)
            out_dve(dve, "down1", 3, O["down1"], None, 0)
            post_dve(dve, PN["final"], gains("final"), N["normA"], first_a, True, 0, 0)
            with dve.Fori(0, LAYERS2) as l:
                dve.tensor_copy(par2[:, :], par2all[:, bass.ds(l, 1), :]).then_inc(*layer_par.one())
                dve.wait_ge(*layer_par.count(1, l))
                for nm in ("postA", "postB"):
                    dve.tensor_scalar(gains2(nm), gains2(nm), 0.5, None, ALU.mult).then_inc(*halved.one())
                up_dve(dve, "upA", FF2, U["upA"], None, N["normA"], l)
                out_dve(dve, "downA", 3, O["downA"], HB, l)
                dve.wait_ge(*halved.count(2, l))
                post_dve(dve, PN["postA"], gains2("postA"), N["normM"], gains2("mpre"), False, l, l)
                hybrid_dve(dve, l)
                out_dve(dve, "w_o", 1, O["w_o"], HB, l)
                post_dve(dve, PN["postM"], gains2("mpost"), N["normB"], gains2("preB"), False, l, l)
                up_dve(dve, "upB", FF2, U["upB"], None, N["normB"], l)
                out_dve(dve, "downB", 3, O["downB"], HB, l)
                post_dve(dve, PN["postB"], gains2("postB"), N["normA"], gains2("nextA"), False, l, l + 1)


def blocks_of(w, ks, cols):
    a = np.stack([w[k * P:(k + 1) * P, c * P:(c + 1) * P] for k in ks for c in cols])
    return a.transpose(1, 0, 2).reshape(P, -1)


def pack_stream(i):
    s = np.zeros((STREAM, P, BLOCKS * P), np.float32)
    at = [0]

    def put(a):
        s[at[0], :, :a.shape[1]] = a
        at[0] += 1

    def pairs(w, cols, groups=(range(KT),)):
        for c in cols:
            for ks in groups:
                put(blocks_of(w, ks, c))

    two = [(2 * g, 2 * g + 1) for g in range(4)]
    w = i["ev_w_in"][0]
    low = np.zeros((D, 2 * P), np.float32)
    low[:, :16] = w[:, 2560:2576]
    w = np.concatenate([w[:, :2560], w[:, 2576:]], axis=1)
    pairs(w, [(2 * g, 2 * g + 1) for g in range(12)])
    pairs(low, [(0, 1)])
    pairs(i["ev_w_out"][0], two)

    def ffn1(l):
        pairs(i["ffn_w_up"][l], [(n, FF1 + n) for n in range(FF1)])
        pairs(i["ffn_w_down"][l], two, (range(0, 8), range(8, 16), range(16, 24)))
    ffn1(0)
    w = i["od_w_in"][0]
    pairs(w, [(8 + 2 * g, 9 + 2 * g) for g in range(4)])
    pairs(w, two)
    wa, wx = i["od_w_a"][0], i["od_w_x"][0]
    for q in range(2):
        part = []
        for j in range(4 * q, 4 * q + 4):
            n, m = divmod(j, 2)
            for k in range(2):
                part += [blocks_of(wa[n], [k], [m]), blocks_of(wx[n], [k], [m])]
        put(np.concatenate(part, axis=1))
    pairs(i["od_w_out"][0], two)
    ffn1(1)
    for l in range(LAYERS2):
        def ffn2(name):
            pairs(i[name + "_w_gate_up_2"][l], [(n, FF2 + n) for n in range(FF2)])
            pairs(i[name + "_w_down_2"][l], two, (range(0, 8), range(8, 16), range(16, 22)))
        ffn2("ffn1")
        w = i["w_in_2"][l]
        pairs(w, two)
        pairs(w, [(24 + 2 * g, 25 + 2 * g) for g in range(4)])
        pairs(w, [(8 + n, 16 + n) for n in range(8)])
        pairs(w, [(32 + n, 40 + n) for n in range(8)])
        pairs(i["w_conv_out_2"][l], two)
        put(np.concatenate([blocks_of(i["w_pool_group_2"][l][g], range(2), range(2)) for g in range(4)], axis=1))
        pairs(i["w_pool_out_2"][l], two)
        pairs(i["w_o_2"][l], two)
        ffn2("ffn2")
    assert at[0] == CHUNKS
    return s


def tiles(v):
    return np.asarray(v).reshape(-1, P).T


def conv_columns(w, order):
    a = np.stack([tiles(t) for t in w], axis=2)
    return a[:, order, :].reshape(P, -1)


def pack_params(i):
    pair = [t for n in range(FF1) for t in (n, FF1 + n)]
    cols = [tiles(i["mix_norm_g"][0]), tiles(i["mix_norm_g"][1]), tiles(i["ffn_norm_g"][0]),
            tiles(i["ffn_norm_g"][1]), tiles(i["final_norm_g"]), tiles(i["ev_b_gk2"][0]),
            tiles(i["ev_gla_norm_g"][0]), conv_columns(i["od_conv_w"][0], list(range(KT))),
            tiles(i["od_conv_b"][0]), tiles(i["od_b_a"][0]), tiles(i["od_b_x"][0]),
            tiles(i["od_lambda"][0])]
    for l in range(2):
        cols += [conv_columns(i["ffn_conv_w"][l], pair), tiles(i["ffn_conv_b"][l])[:, pair]]
    par1 = np.concatenate(cols, axis=1)
    par2 = np.stack([np.concatenate(
        [tiles(i["ffn1_pre_2"][(l + 1) % LAYERS2])] +
        [tiles(i[n + "_2"][l]) for n in ("ffn1_pre", "ffn1_post", "mix_pre", "mix_post", "ffn2_pre",
                                         "ffn2_post", "b_gate")]
        + [conv_columns(i["conv_w_2"][l], list(range(KT))), tiles(i["b_pool_group_2"][l]),
           tiles(i["pool_scale_2"][l])], axis=1) for l in range(LAYERS2)], axis=1)
    return par1, par2


def constants(wgk2):
    half_ = 32
    inv = (np.float32(10000.0) ** (-np.arange(half_, dtype=np.float32) / np.float32(half_))).astype(np.float32)
    ang = (np.arange(T, dtype=np.float32)[None, :] * inv[:, None]).astype(np.float32).astype(np.float64)
    cos, sin = np.cos(ang).astype(np.float32), np.sin(ang).astype(np.float32)
    ev = np.zeros((P, 4, T), np.float32)
    ev[:, 0] = np.tile(cos, (4, 1))
    ev[:, 1] = np.concatenate([-sin, sin, -sin, sin])
    for m in range(P):
        ev[m ^ 32, 2, m] = 1.0
    ev[0:16, 3, :] = wgk2
    q, k = np.arange(P)[:, None], np.arange(P)[None, :]
    masks = np.zeros((P, 6, T), np.float32)
    mb = masks[:, 0:2].reshape(P, 2 * T)
    mb[:, 0:P] = mb[:, 2 * P:3 * P] = np.where(k <= q, 0.0, -1e30)
    masks[:, 0:2] = mb.reshape(P, 2, T)
    lv = np.zeros((P, LEVELS, P), np.uint32)
    s, t = q, k
    lv[:, 0] = s == t
    for i in range(1, LEVELS):
        n = 2 ** (i - 1)
        lv[:, i] = (s // (2 * n) == t // (2 * n)) & (s // n % 2 == 0) & (t // n % 2 == 1)
    masks[:, 2:6] = lv.view(np.float32).reshape(P, 4, T)
    mats = np.zeros((P, 3, P), np.float32)
    mats[:, 0] = np.eye(P)
    mats[:, 1] = 1.0 / D
    mats[:, 2] = (q // 64 == k // 64) / 64.0
    winv = np.stack([1.0 / np.minimum(np.arange(1, T + 1), 2 ** (g + 1)) for g in range(4)]).astype(np.float32)
    return ev, masks, mats, np.broadcast_to(winv, (P, 4, T)).copy()


def kernel(**inputs):
    import concourse.bacc as bacc
    from concourse.bass_utils import run_bass_kernel_spmd

    i = {k: np.asarray(v) for k, v in inputs.items()}
    par1, par2 = pack_params(i)
    ev, masks, mats, winv = constants(i["ev_w_gk2"][0])
    arrays = {
        "x_in": np.ascontiguousarray(i["x"][0].T.reshape(KT, P, T).transpose(1, 0, 2)),
        "stream_in": pack_stream(i), "par1_in": np.ascontiguousarray(par1),
        "par2_in": np.ascontiguousarray(par2), "ev_in": ev, "mask_in": masks, "mat_in": mats,
        "inv_in": winv,
    }
    nc = bacc.Bacc("TRN2", target_bir_lowering=False, num_devices=1)
    args = [nc.dram_tensor(n, a.shape, F32, kind="ExternalInput").ap() for n, a in arrays.items()]
    out = nc.dram_tensor("y_out", (P, KT, T), F32, kind="ExternalOutput").ap()
    program(nc, *args, out)
    r = run_bass_kernel_spmd(nc, [arrays], core_ids=[0])
    y = r.results[0]["y_out"]
    return np.ascontiguousarray(y.transpose(2, 1, 0).reshape(1, T, D))
```
